# Optimizing a Trainium2 kernel written in Bass

```python
import math
import jax, jax.numpy as jnp
from jax import lax
import numpy as np

D_MODEL = 1024
BATCH = 1
SEQ = 256
DEPTH = 2

HEAD_DIM = 64
GROUP_W = D_MODEL // 4
MIX_W = 4 * GROUP_W
DIFF_HEADS = GROUP_W // HEAD_DIM
DIFF_QK_DIM = HEAD_DIM // 2
CONV_W = GROUP_W
CONV_KERNEL = 31
GMLP_HEADS = GROUP_W // HEAD_DIM
GMLP_W = GROUP_W
CHUNK = 128
FOX_HEADS = GROUP_W // HEAD_DIM
FOX_W = GROUP_W
D_FF = ((8 * D_MODEL // 3 + 127) // 128) * 128
Q_BLOCK = 128
N_MOD = 9
EPS = 1e-6
NEG_INF = -1e30

DIFF_Q0 = 0
DIFF_K0 = DIFF_Q0 + DIFF_HEADS * 2 * DIFF_QK_DIM
DIFF_V0 = DIFF_K0 + DIFF_HEADS * 2 * DIFF_QK_DIM
CONV0 = DIFF_V0 + DIFF_HEADS * HEAD_DIM
GMLP0 = CONV0 + 2 * CONV_W
FOX_Q0 = GMLP0 + 2 * GMLP_W
FOX_K0 = FOX_Q0 + FOX_W
FOX_V0 = FOX_K0 + FOX_W
FOX_F0 = FOX_V0 + FOX_W
IN_COLS = FOX_F0 + FOX_HEADS


def _rms_norm(x, g):
    xf = x.astype(jnp.float32)
    y = xf * lax.rsqrt(jnp.mean(xf * xf, axis=-1, keepdims=True) + EPS)
    return (y * g.astype(jnp.float32)).astype(x.dtype)

def _layer_norm(x, g, b):
    xf = x.astype(jnp.float32)
    mu = jnp.mean(xf, axis=-1, keepdims=True)
    var = jnp.mean(jnp.square(xf - mu), axis=-1, keepdims=True)
    y = (xf - mu) * lax.rsqrt(var + EPS)
    return (y * g.astype(jnp.float32) + b.astype(jnp.float32)).astype(x.dtype)

def _modulate(xn, shift, scale):
    return xn * (1 + scale[:, None, :]) + shift[:, None, :]

def _swiglu(x, w_in, w_out):
    gate, up = jnp.split(x @ w_in, 2, axis=-1)
    return (jax.nn.silu(gate) * up) @ w_out

def _differential_attention(q, k, v, lam, lam_init, out_g):
    B, S, H, _, dq = q.shape
    dv = v.shape[-1]
    nb = S // Q_BLOCK
    q_blocks = jnp.moveaxis(q.reshape(B, nb, Q_BLOCK, H, 2, dq), 1, 0)
    k_pos = jnp.arange(S)
    scale = dq ** -0.5

    def one_block(args):
        qi, i = args
        s = jnp.einsum('bqhcd,bkhcd->bhcqk', qi, k).astype(jnp.float32) * scale
        q_pos = i * Q_BLOCK + jnp.arange(Q_BLOCK)
        causal = k_pos[None, :] <= q_pos[:, None]
        p = jax.nn.softmax(jnp.where(causal, s, NEG_INF), axis=-1)
        a = p[:, :, 0] - lam * p[:, :, 1]
        return jnp.einsum('bhqk,bkhe->bqhe', a.astype(v.dtype), v)

    o = lax.map(one_block, (q_blocks, jnp.arange(nb)))
    o = jnp.moveaxis(o, 0, 1).reshape(B, S, H, dv)
    o = _rms_norm(o, out_g) * (1.0 - lam_init)
    return o.reshape(B, S, H * dv)

def _conformer_conv(z, w, b, ng, nb_):
    a, g = jnp.split(z, 2, axis=-1)
    y = a * jax.nn.sigmoid(g)
    y = lax.conv_general_dilated(
        y, w[:, None, :].astype(y.dtype), window_strides=(1,),
        padding=[(CONV_KERNEL - 1, 0)],
        dimension_numbers=('NWC', 'WIO', 'NWC'),
        feature_group_count=CONV_W) + b
    return jax.nn.silu(_layer_norm(y, ng, nb_))

def _chunked_spatial_gating(z, ng, nb_, ws, bs):
    u, v = jnp.split(jax.nn.gelu(z), 2, axis=-1)
    v = _layer_norm(v, ng, nb_)
    B, S, _ = v.shape
    nc = S // CHUNK
    vh = v.reshape(B, nc, CHUNK, GMLP_HEADS, HEAD_DIM)
    w = ws * jnp.tril(jnp.ones((CHUNK, CHUNK), ws.dtype))[None]
    s = jnp.einsum('hts,bnshd->bnthd', w, vh) + jnp.transpose(bs)[None, None, :, :, None]
    return u * s.reshape(B, S, GMLP_W)

def _forgetting_attention(q, k, v, log_f):
    B, S, H, d = q.shape
    nb = S // Q_BLOCK
    cum = jnp.cumsum(log_f.astype(jnp.float32), axis=1)
    q_blocks = jnp.moveaxis(q.reshape(B, nb, Q_BLOCK, H, d), 1, 0)
    c_blocks = jnp.moveaxis(cum.reshape(B, nb, Q_BLOCK, H), 1, 0)
    cum_k = jnp.transpose(cum, (0, 2, 1))
    k_pos = jnp.arange(S)
    scale = d ** -0.5

    def one_block(args):
        qi, ci, i = args
        s = jnp.einsum('bqhd,bkhd->bhqk', qi, k).astype(jnp.float32) * scale
        s = s + jnp.transpose(ci, (0, 2, 1))[..., None] - cum_k[:, :, None, :]
        q_pos = i * Q_BLOCK + jnp.arange(Q_BLOCK)
        causal = k_pos[None, :] <= q_pos[:, None]
        p = jax.nn.softmax(jnp.where(causal, s, NEG_INF), axis=-1)
        return jnp.einsum('bhqk,bkhd->bqhd', p.astype(v.dtype), v)

    o = lax.map(one_block, (q_blocks, c_blocks, jnp.arange(nb)))
    return jnp.moveaxis(o, 0, 1).reshape(B, S, H * d)

def first_inputs(seed: int = 0) -> dict:
    key = jax.random.key(seed)
    ks = jax.random.split(key, 24)
    f32 = jnp.float32

    def nrm(k, shape, s):
        return jax.random.normal(k, shape, f32) * s

    L = DEPTH
    return {
        'x': nrm(ks[0], (BATCH, SEQ, D_MODEL), 1.0),
        'c': nrm(ks[1], (BATCH, D_MODEL), 1.0),
        'ada_w': nrm(ks[2], (L, D_MODEL, N_MOD * D_MODEL), 0.5 * D_MODEL ** -0.5),
        'ada_b': nrm(ks[3], (L, N_MOD * D_MODEL), 0.02),
        'norm_g': 1.0 + nrm(ks[4], (L, 3, D_MODEL), 0.05),
        'ffn1_w_in': nrm(ks[5], (L, D_MODEL, 2 * D_FF), D_MODEL ** -0.5),
        'ffn1_w_out': nrm(ks[6], (L, D_FF, D_MODEL), D_FF ** -0.5),
        'ffn2_w_in': nrm(ks[7], (L, D_MODEL, 2 * D_FF), D_MODEL ** -0.5),
        'ffn2_w_out': nrm(ks[8], (L, D_FF, D_MODEL), D_FF ** -0.5),
        'w_in': nrm(ks[9], (L, D_MODEL, IN_COLS), D_MODEL ** -0.5),
        'w_out': nrm(ks[10], (L, MIX_W, D_MODEL), MIX_W ** -0.5),
        'diff_qk_g': 1.0 + nrm(ks[11], (L, 2, DIFF_QK_DIM), 0.05),
        'diff_lambda': nrm(ks[12], (L, 4, DIFF_QK_DIM), 0.1),
        'diff_out_g': 1.0 + nrm(ks[13], (L, HEAD_DIM), 0.05),
        'conv_w': nrm(ks[14], (L, CONV_KERNEL, CONV_W), CONV_KERNEL ** -0.5),
        'conv_b': nrm(ks[15], (L, CONV_W), 0.02),
        'conv_norm_g': 1.0 + nrm(ks[16], (L, CONV_W), 0.05),
        'conv_norm_b': nrm(ks[17], (L, CONV_W), 0.02),
        'gmlp_norm_g': 1.0 + nrm(ks[18], (L, GMLP_W), 0.05),
        'gmlp_norm_b': nrm(ks[19], (L, GMLP_W), 0.02),
        'gmlp_ws': nrm(ks[20], (L, GMLP_HEADS, CHUNK, CHUNK), CHUNK ** -0.5),
        'gmlp_bs': 1.0 + nrm(ks[21], (L, GMLP_HEADS, CHUNK), 0.1),
        'fox_qk_g': 1.0 + nrm(ks[22], (L, 2, HEAD_DIM), 0.05),
        'fox_fb': 2.0 + nrm(ks[23], (L, FOX_HEADS), 0.5),
    }

def first_block(x, c, ada_w, ada_b, norm_g, ffn1_w_in, ffn1_w_out, ffn2_w_in, ffn2_w_out,
              w_in, w_out, diff_qk_g, diff_lambda, diff_out_g, conv_w, conv_b,
              conv_norm_g, conv_norm_b, gmlp_norm_g, gmlp_norm_b, gmlp_ws, gmlp_bs,
              fox_qk_g, fox_fb):
    B, S, _ = x.shape
    h = x
    cond = jax.nn.silu(c)
    for l in range(DEPTH):
        mod = cond @ ada_w[l] + ada_b[l]
        sh1, sc1, g1, sh2, sc2, g2, sh3, sc3, g3 = jnp.split(mod, N_MOD, axis=-1)

        hn = _modulate(_rms_norm(h, norm_g[l, 0]), sh1, sc1)
        h = h + 0.5 * g1[:, None, :] * _swiglu(hn, ffn1_w_in[l], ffn1_w_out[l])

        hn = _modulate(_rms_norm(h, norm_g[l, 1]), sh2, sc2)
        z = hn @ w_in[l]

        qa = _rms_norm(z[..., DIFF_Q0:DIFF_K0].reshape(B, S, DIFF_HEADS, 2, DIFF_QK_DIM), diff_qk_g[l, 0])
        ka = _rms_norm(z[..., DIFF_K0:DIFF_V0].reshape(B, S, DIFF_HEADS, 2, DIFF_QK_DIM), diff_qk_g[l, 1])
        va = z[..., DIFF_V0:CONV0].reshape(B, S, DIFF_HEADS, HEAD_DIM)
        lam_init = 0.8 - 0.6 * math.exp(-0.3 * l)
        lv = diff_lambda[l].astype(jnp.float32)
        lam = jnp.exp(jnp.sum(lv[0] * lv[1])) - jnp.exp(jnp.sum(lv[2] * lv[3])) + lam_init
        o_a = _differential_attention(qa, ka, va, lam, lam_init, diff_out_g[l])

        o_b = _conformer_conv(z[..., CONV0:GMLP0], conv_w[l], conv_b[l], conv_norm_g[l], conv_norm_b[l])

        o_c = _chunked_spatial_gating(z[..., GMLP0:FOX_Q0], gmlp_norm_g[l], gmlp_norm_b[l], gmlp_ws[l], gmlp_bs[l])

        qd = _rms_norm(z[..., FOX_Q0:FOX_K0].reshape(B, S, FOX_HEADS, HEAD_DIM), fox_qk_g[l, 0])
        kd = _rms_norm(z[..., FOX_K0:FOX_V0].reshape(B, S, FOX_HEADS, HEAD_DIM), fox_qk_g[l, 1])
        vd = z[..., FOX_V0:FOX_F0].reshape(B, S, FOX_HEADS, HEAD_DIM)
        log_f = jax.nn.log_sigmoid((z[..., FOX_F0:IN_COLS] + fox_fb[l]).astype(jnp.float32))
        o_d = _forgetting_attention(qd, kd, vd, log_f)

        mixed = jnp.concatenate([o_a, o_b, o_c, o_d], axis=-1)
        h = h + g2[:, None, :] * (mixed @ w_out[l])

        hn = _modulate(_rms_norm(h, norm_g[l, 2]), sh3, sc3)
        h = h + 0.5 * g3[:, None, :] * _swiglu(hn, ffn2_w_in[l], ffn2_w_out[l])
    return h


HG_HEADS = 4
HG_DK = 128
HG_DV = 128
HG_WIDTH = HG_HEADS * HG_DK
HG_CHUNK = 64
AT_HEADS = 8
AT_KV_HEADS = 2
AT_HEAD_DIM = 64
AT_WIDTH = AT_HEADS * AT_HEAD_DIM
AT_KV_WIDTH = AT_KV_HEADS * AT_HEAD_DIM
WINDOW = 128
ATT_BLOCK = 128
N_BRANCH = 2
D_FF_2 = 2816
N_NORMS = 6
IN_SIZES = (HG_WIDTH, HG_WIDTH, HG_WIDTH, HG_WIDTH,
            AT_WIDTH, AT_KV_WIDTH, AT_KV_WIDTH, D_MODEL, D_MODEL)
D_IN = sum(IN_SIZES)
IN_SPLITS = tuple(int(v) for v in np.cumsum(IN_SIZES)[:-1])


def rms_norm(x, gain):
    xf = x.astype(jnp.float32)
    y = xf * lax.rsqrt(jnp.mean(xf * xf, axis=-1, keepdims=True) + EPS)
    return (y * gain.astype(jnp.float32)).astype(x.dtype)

def swiglu(h, w_gate, w_up, w_down):
    return (jax.nn.silu(h @ w_gate) * (h @ w_up)) @ w_down

def alibi_slopes(n_heads):
    idx = jnp.arange(1, n_heads + 1, dtype=jnp.float32)
    return jnp.exp2(-8.0 * idx / n_heads)

def hgrn2_mixer(q, f_logit, i, g_out, lb, head_gain):
    B, S, _ = q.shape
    dt = q.dtype
    nc = S // HG_CHUNK
    lb = lb.astype(jnp.float32)
    z = f_logit.astype(jnp.float32)
    log_f = jnp.logaddexp(jnp.log(lb), jnp.log1p(-lb) + jax.nn.log_sigmoid(z))
    k = (1.0 - lb) * jax.nn.sigmoid(-z)
    qf = jax.nn.silu(q.astype(jnp.float32))
    vf = i.astype(jnp.float32)

    def to_chunks(t, d):
        return t.reshape(B, nc, HG_CHUNK, HG_HEADS, d).transpose(1, 0, 3, 2, 4)

    qc, kc, vc, gc = (to_chunks(qf, HG_DK), to_chunks(k, HG_DK),
                      to_chunks(vf, HG_DV), to_chunks(log_f, HG_DK))
    causal = jnp.tril(jnp.ones((HG_CHUNK, HG_CHUNK), dtype=bool))

    def step(state, inp):
        qb, kb, vb, gb = inp
        G = jnp.cumsum(gb, axis=2)
        o_inter = jnp.einsum('bhtd,bhde->bhte', qb * jnp.exp(G), state)
        diff = G[:, :, :, None, :] - G[:, :, None, :, :]
        decay = jnp.exp(jnp.where(causal[:, :, None], diff, -jnp.inf))
        scores = jnp.einsum('bhtd,bhtsd,bhsd->bhts', qb, decay, kb)
        o = o_inter + jnp.einsum('bhts,bhse->bhte', scores, vb)
        G_last = G[:, :, -1:, :]
        new_state = (jnp.exp(G_last[:, :, 0, :])[..., None] * state
                     + jnp.einsum('bhsd,bhse->bhde', kb * jnp.exp(G_last - G), vb))
        return new_state, o

    state0 = jnp.zeros((B, HG_HEADS, HG_DK, HG_DV), jnp.float32)
    _, o = lax.scan(step, state0, (qc, kc, vc, gc))
    o = o.transpose(1, 0, 3, 2, 4).reshape(B, S, HG_HEADS, HG_DV)
    o = o * lax.rsqrt(jnp.mean(o * o, axis=-1, keepdims=True) + EPS) * head_gain.astype(jnp.float32)
    o = o.reshape(B, S, HG_WIDTH) * jax.nn.silu(g_out.astype(jnp.float32))
    return o.astype(dt)

def swa_sink_attention(q, k, v, sinks):
    B, S, _ = q.shape
    dt = q.dtype
    L = ATT_BLOCK
    nb = S // L
    G = AT_HEADS // AT_KV_HEADS
    qb = q.reshape(B, nb, L, AT_KV_HEADS, G, AT_HEAD_DIM)
    kb = k.reshape(B, nb, L, AT_KV_HEADS, AT_HEAD_DIM)
    vb = v.reshape(B, nb, L, AT_KV_HEADS, AT_HEAD_DIM)
    pad = ((0, 0), (1, 0), (0, 0), (0, 0), (0, 0))
    kk = jnp.concatenate([jnp.pad(kb[:, :-1], pad), kb], axis=2)
    vv = jnp.concatenate([jnp.pad(vb[:, :-1], pad), vb], axis=2)
    s = jnp.einsum('bnqhgd,bnkhd->bnhgqk', qb, kk).astype(jnp.float32) * (AT_HEAD_DIM ** -0.5)
    qi = jnp.arange(L)[:, None] + L
    kj = jnp.arange(2 * L)[None, :]
    dist = qi - kj
    in_window = (dist >= 0) & (dist < WINDOW)
    key_exists = (jnp.arange(nb)[:, None] * L + kj - L) >= 0
    mask = in_window[None] & key_exists[:, None, :]
    slopes = alibi_slopes(AT_HEADS).reshape(AT_KV_HEADS, G)
    s = s - slopes[:, :, None, None] * dist.astype(jnp.float32)
    s = jnp.where(mask[None, :, None, None], s, -jnp.inf)
    sink = jnp.broadcast_to(sinks.astype(jnp.float32).reshape(AT_KV_HEADS, G)[None, None, :, :, None, None],
                            s.shape[:-1] + (1,))
    p = jax.nn.softmax(jnp.concatenate([s, sink], axis=-1), axis=-1)[..., :-1]
    out = jnp.einsum('bnhgqk,bnkhd->bnqhgd', p.astype(dt), vv)
    return out.reshape(B, S, AT_WIDTH)

def second_inputs(seed: int = 0) -> dict:
    key = jax.random.key(seed)
    ks = jax.random.split(key, 16)
    f32 = jnp.float32

    def w(k, shape, fan_in):
        return jax.random.normal(k, shape, f32) * (fan_in ** -0.5)

    return {
        "x": jax.random.normal(ks[0], (BATCH, SEQ, D_MODEL), f32),
        "norm_gains": 1.0 + 0.1 * jax.random.normal(ks[1], (DEPTH, N_NORMS, D_MODEL), f32),
        "w_ffn1_gate": w(ks[2], (DEPTH, D_MODEL, D_FF_2), D_MODEL),
        "w_ffn1_up": w(ks[3], (DEPTH, D_MODEL, D_FF_2), D_MODEL),
        "w_ffn1_down": w(ks[4], (DEPTH, D_FF_2, D_MODEL), D_FF_2),
        "w_in": w(ks[5], (DEPTH, D_MODEL, D_IN), D_MODEL),
        "hgrn_lower_bounds": jax.random.normal(ks[6], (DEPTH, HG_WIDTH), f32),
        "hgrn_head_gain": 1.0 + 0.1 * jax.random.normal(ks[7], (DEPTH, HG_DV), f32),
        "attn_sinks": 0.5 * jax.random.normal(ks[8], (DEPTH, AT_HEADS), f32),
        "w_branch_hgrn": w(ks[9], (DEPTH, HG_WIDTH, D_MODEL), HG_WIDTH),
        "w_branch_attn": w(ks[10], (DEPTH, AT_WIDTH, D_MODEL), AT_WIDTH),
        "w_out": w(ks[11], (DEPTH, D_MODEL, D_MODEL), D_MODEL),
        "w_ffn2_gate": w(ks[12], (DEPTH, D_MODEL, D_FF_2), D_MODEL),
        "w_ffn2_up": w(ks[13], (DEPTH, D_MODEL, D_FF_2), D_MODEL),
        "w_ffn2_down": w(ks[14], (DEPTH, D_FF_2, D_MODEL), D_FF_2),
    }

def second_block(x, norm_gains, w_ffn1_gate, w_ffn1_up, w_ffn1_down, w_in, hgrn_lower_bounds,
              hgrn_head_gain, attn_sinks, w_branch_hgrn, w_branch_attn, w_out,
              w_ffn2_gate, w_ffn2_up, w_ffn2_down):
    lb_all = jnp.cumsum(jax.nn.softmax(hgrn_lower_bounds.astype(jnp.float32), axis=0), axis=0)
    lb_all = lb_all - lb_all[0:1]
    for l in range(DEPTH):
        gn = norm_gains[l]
        h = rms_norm(x, gn[0])
        x = x + 0.5 * rms_norm(swiglu(h, w_ffn1_gate[l], w_ffn1_up[l], w_ffn1_down[l]), gn[1])
        h = rms_norm(x, gn[2])
        proj = h @ w_in[l]
        hq, hf, hi, hg, aq, ak, av, gate_a, gate_b = jnp.split(proj, IN_SPLITS, axis=-1)
        y_hg = hgrn2_mixer(hq, hf, hi, hg, lb_all[l], hgrn_head_gain[l]) @ w_branch_hgrn[l]
        y_at = swa_sink_attention(aq, ak, av, attn_sinks[l]) @ w_branch_attn[l]
        mixed = jax.nn.sigmoid(gate_a) * y_hg + jax.nn.sigmoid(gate_b) * y_at
        x = x + rms_norm(mixed @ w_out[l], gn[3])
        h = rms_norm(x, gn[4])
        x = x + 0.5 * rms_norm(swiglu(h, w_ffn2_gate[l], w_ffn2_up[l], w_ffn2_down[l]), gn[5])
    return x


def setup_inputs(seed=0):
    out = dict(first_inputs(seed))
    for name, value in second_inputs(seed + 1).items():
        if name != "x":
            out[name + "_2"] = value
    return out


def reference(
    x, c, ada_w, ada_b, norm_g, ffn1_w_in, ffn1_w_out, ffn2_w_in, ffn2_w_out, w_in, w_out,
    diff_qk_g, diff_lambda, diff_out_g, conv_w, conv_b, conv_norm_g, conv_norm_b, gmlp_norm_g,
    gmlp_norm_b, gmlp_ws, gmlp_bs, fox_qk_g, fox_fb, norm_gains_2, w_ffn1_gate_2, w_ffn1_up_2,
    w_ffn1_down_2, w_in_2, hgrn_lower_bounds_2, hgrn_head_gain_2, attn_sinks_2, w_branch_hgrn_2,
    w_branch_attn_2, w_out_2, w_ffn2_gate_2, w_ffn2_up_2, w_ffn2_down_2,
):
    x = first_block(
        x, c, ada_w, ada_b, norm_g, ffn1_w_in, ffn1_w_out, ffn2_w_in, ffn2_w_out, w_in, w_out,
        diff_qk_g, diff_lambda, diff_out_g, conv_w, conv_b, conv_norm_g, conv_norm_b,
        gmlp_norm_g, gmlp_norm_b, gmlp_ws, gmlp_bs, fox_qk_g, fox_fb,
    )
    return second_block(
        x, norm_gains_2, w_ffn1_gate_2, w_ffn1_up_2, w_ffn1_down_2, w_in_2, hgrn_lower_bounds_2,
        hgrn_head_gain_2, attn_sinks_2, w_branch_hgrn_2, w_branch_attn_2, w_out_2,
        w_ffn2_gate_2, w_ffn2_up_2, w_ffn2_down_2,
    )


_drawn_inputs = setup_inputs


def setup_inputs(seed=0):
    import zlib

    import numpy as np

    out = dict(_drawn_inputs(seed))
    spreads = {}
    factors = {'diff_qk_g': 5.321,
     'diff_out_g': 3.071,
     'conv_b': 4.621,
     'conv_norm_g': 3.65,
     'conv_norm_b': 8.0,
     'gmlp_norm_g': 7.01,
     'gmlp_norm_b': 8.0,
     'fox_qk_g': 8.0}
    for name, (base, spread) in spreads.items():
        noise = np.random.default_rng([zlib.crc32(name.encode()), seed]).standard_normal(out[name].shape)
        drawn = base * np.exp(spread * noise) if base else spread * noise
        out[name] = __import__('jax').numpy.asarray(drawn.astype(out[name].dtype))
    for name, factor in factors.items():
        out[name] = (out[name] * factor).astype(out[name].dtype)
    return out
```

```python
from contextlib import ExitStack

import concourse.bass as bass
from concourse import mybir

ALU = mybir.AluOpType
ACT = mybir.ActivationFunctionType
AX = mybir.AxisListType
F32 = mybir.dt.float32
F32R = mybir.dt.float32r
BF16 = mybir.dt.bfloat16
I32 = mybir.dt.int32
U8 = mybir.dt.uint8

P = 128
EPS = 1e-6
NEG = -1e30
GELU_A = 0.044715
GELU_B = -2.0 * 0.7978845608028654
LAM_INIT = (0.8 - 0.6, 0.8 - 0.6 * 0.7408182206817179)

PARTS = (('ffn', 'mix', 'ffn'), ('ffn', 'mix', 'ffn'))
DVE_STEPS = (74, 80)
ACT_STEPS = (10, 11)
PE_STEPS = (5, 0)
EVENTS_OF = {("ffn", 0): 1, ("mix", 0): 5, ("ffn", 1): 2, ("mix", 1): 3}
EVENTS = tuple(sum(EVENTS_OF[(p, b)] for p in PARTS[b]) for b in range(2))


class Steps:

    def __init__(self, eng, sem, l=0, per_layer=0):
        self.eng, self.sem, self.base, self.k = eng, sem, l * per_layer, 0

    def __call__(self, ins):
        ins.then_inc(self.sem, 1)
        self.k += 1
        self.eng.wait_ge(self.sem, self.base + self.k)


def program(nc, x, c, ada_w, ada_b, norm_g, ffn1_w_in, ffn1_w_out, ffn2_w_in, ffn2_w_out, w_in, w_out,
            diff_qk_g, diff_lambda, diff_out_g, conv_w, conv_b, conv_norm_g, conv_norm_b, gmlp_norm_g,
            gmlp_norm_b, gmlp_ws, gmlp_bs, fox_qk_g, fox_fb, norm_gains_2, w_ffn1_gate_2, w_ffn1_up_2,
            w_ffn1_down_2, w_in_2, hgrn_lower_bounds_2, hgrn_head_gain_2, attn_sinks_2, w_branch_hgrn_2,
            w_branch_attn_2, w_out_2, w_ffn2_gate_2, w_ffn2_up_2, w_ffn2_down_2, out):
    LAYERS, D, NADA = ada_w.shape
    S = x.shape[1]
    KC = D // P
    DFF = ffn1_w_out.shape[1]
    GROUPS = DFF // 256
    UNIT = 2048
    LOADED = 64
    CONVK = conv_w.shape[1]
    FFN_UNITS = 3 * GROUPS
    UNITS = {("ffn", 0): FFN_UNITS, ("ffn", 1): FFN_UNITS, ("mix", 0): 15, ("mix", 1): 27}
    NU = [sum(UNITS[(p, b)] for p in PARTS[b]) for b in range(2)]
    assert all(n % 3 == 0 for n in NU) and S == 256 and D == 1024

    with ExitStack() as ctx:
        def sb(name, shape, dt=F32):
            return ctx.enter_context(nc.sbuf_tensor(name, shape, dt))

        hT = sb("hT", [P, KC, S])
        raw = sb("raw", [P, 3, UNIT])
        whi = sb("whi", [P, 3, UNIT], F32R)
        wlo = sb("wlo", [P, 3, UNIT], F32R)
        xh = sb("xh", [P, KC, S], F32R)
        xl = sb("xl", [P, KC, S], F32R)
        hidh = sb("hidh", [P, 2 * S], F32R)
        hidl = sb("hidl", [P, 2 * S], F32R)
        sq8 = sb("sq8", [P, 2048])
        u8 = sb("u8", [P, 2048])
        nrm = sb("nrm", [P, 3, S])
        ident = sb("ident", [P, P])
        ones_d = sb("ones_d", [P, P])
        ones_128 = sb("ones_128", [P, P])
        blk64 = sb("blk64", [P, P])
        blk32 = sb("blk32", [P, P])
        ones_col = sb("ones_col", [P, 2])
        ones_row = sb("ones_row", [P, P])
        zerow = sb("zerow", [P, 512], BF16)
        amask = sb("amask", [P, 384])
        wmask = sb("wmask", [P, 384])
        dist = sb("dist", [P, 384])
        hmask = sb("hmask", [P, 8, P], U8)
        epsc = sb("epsc", [P, 1])
        prm = sb("prm", [P, 512])
        condT = sb("condT", [P, 3, KC])
        foxg = sb("foxg", [P, 4])
        diffg = sb("diffg", [P, 4])
        dog = sb("dog", [P, 2])
        fb = sb("fb", [4, 2])
        sinkb = sb("sinkb", [P, 16])
        lamb = sb("lamb", [P, 12])
        lbt = sb("lbt", [P, 6, 4])
        lbc = sb("lbc", [P, 2, 4])
        la = sb("la", [P, 2, 4])
        l1 = sb("l1", [P, 2, 4])
        ngb = sb("ngb", [P, 2, 2, 256])
        bsb = sb("bsb", [P, 2, 2, P])
        mod = sb("mod", [P, 24])
        gA = sb("gA", [P, 8])
        gB = sb("gB", [P, 8])
        gG = sb("gG", [P, 8])
        mx = sb("mx", [P, 8])
        nmx = sb("nmx", [P, 8])
        ssum = sb("ssum", [P, 8])
        rsum = sb("rsum", [P, 8])
        sinke = sb("sinke", [P, 8])
        lnst = sb("lnst", [P, 2, 6])
        lnmv = sb("lnmv", [P, 2, 2])
        lnr = sb("lnr", [P, 4, 2])
        condk = sb("condk", [P, 1])
        adaT = sb("adaT", [P, 2, 512])
        ARENA = 16448
        arena = sb("arena", [P, ARENA])

        class Carve:
            def __init__(self):
                self.at = 0

            def __call__(self, *shape):
                n = 1
                for s in shape:
                    n *= s
                ap = arena[:, self.at:self.at + n]
                self.at += n
                assert self.at <= ARENA, self.at
                if len(shape) == 2:
                    ap = ap.rearrange("p (a b) -> p a b", a=shape[0])
                if len(shape) == 3:
                    ap = ap.rearrange("p (a b c) -> p a b c", a=shape[0], b=shape[1])
                return ap

        c1 = Carve()
        acc = c1(2, 3072)
        Z = c1(11, 512)
        ypad = c1(2, S + CONVK - 1)
        S0 = c1(4, 384)
        gcum = c1(2, S)
        sel = c1(4, S)
        c1.at = ARENA - 1024
        wsT = c1(8, P)
        assert c1.at <= ARENA
        adaf = arena[:, 6144:6144 + 3 * 3072].rearrange("p (a b) -> p a b", a=3)
        adam = arena[:, 6144:6144 + 3072]
        stage = arena[:, 6144 + 3 * 3072:6144 + 3 * 3072 + 512].rearrange("p (a b) -> p a b", a=4)
        wsn = arena[:, 3072:3072 + 1024].rearrange("p (a b) -> p a b", a=8)
        lraw = arena[:, 3072 + 1024:3072 + 1280].rearrange("p (a b) -> p a b", a=8)
        lprod = arena[:, 3072 + 1280:3072 + 1408].rearrange("p (a b) -> p a b", a=4)
        iot = arena[:, 3072 + 1408:3072 + 1792].bitcast(I32)
        c2 = Carve()
        HQ, HG, HF, HK = c2(4, S), c2(4, S), c2(4, S), c2(4, S)
        HQG = arena[:, 0:2048]
        HC = c2(4, S)
        HV = c2(2, 512)
        AQ = c2(4, S)
        AK = c2(S)
        AV = c2(2, P)
        GA = c2(16, S)
        AT = c2(12, P)
        S1 = u8[:, 0:1536].rearrange("p (h k) -> p h k", h=4)
        PT1 = sq8[:, 0:1536]

        ps = ctx.enter_context(nc.psum_tensor("ps", [P, 8, 512], F32))
        G_BANK, U_BANK, ACC, PVB, STAT = 0, 1, 2, 5, 6

        def sem(name):
            return ctx.enter_context(nc.semaphore(name))

        raw_loaded = [sem(f"raw_loaded{i}") for i in range(3)]
        hi_done, lo_done, unit_used = sem("hi_done"), sem("lo_done"), sem("unit_used")
        x_loaded, stage_loaded, smalls_loaded = sem("x_loaded"), sem("stage_loaded"), sem("smalls_loaded")
        ada0_loaded = [sem(f"ada0_loaded{i}") for i in range(3)]
        ada0_used = sem("ada0_used")
        ada_loaded = [sem(f"ada_loaded{i}") for i in range(2)]
        pool_waited, sp_waited, dve_waited = sem("pool_waited"), sem("sp_waited"), sem("dve_waited")
        ada_zeroed, condk_ready = sem("ada_zeroed"), sem("condk_ready")
        ada_scaled, ada_added = sem("ada_scaled"), sem("ada_added")
        ada_ready, mod_summed = [sem(f"ada_ready{j}") for j in range(3)], sem("mod_summed")
        ada1_loaded, ada1_used, acc_zeroed = sem("ada1_loaded"), sem("ada1_used"), sem("acc_zeroed")
        consts_ready, dconsts_ready = sem("consts_ready"), sem("dconsts_ready")
        stage_turned, prm_ready, cond_ready = sem("stage_turned"), sem("prm_ready"), sem("cond_ready")
        x_turned, h_ready = sem("x_turned"), sem("h_ready")
        ws_turned, ws_ready = sem("ws_turned"), sem("ws_ready")
        dve_step = [sem("dve_step0"), sem("dve_step1")]
        pe_step = [sem("pe_step0"), sem("pe_step1")]
        act_step = [sem("act_step0"), sem("act_step1")]
        dve_setup, act_setup, pool_step = sem("dve_setup"), sem("act_setup"), sem("pool_step")
        acc_done = sem("acc_done")
        nsq_ready, ms_ready, y_ready = sem("nsq_ready"), sem("ms_ready"), sem("y_ready")
        u_ready, xh_ready, x_ready = sem("u_ready"), sem("xh_ready"), sem("x_ready")
        sig_ready = sem("sig_ready")
        prod_ready, h32_ready = sem("prod_ready"), sem("h32_ready")
        hidh_ready, hid_ready = sem("hidh_ready"), sem("hid_ready")
        z_copied = [sem("z_copied0"), sem("z_copied1")]
        mix_names = ("convexp", "conv_in", "conv_done", "foxqk_sq", "foxqk_r", "foxqk", "diffqk_sq", "diffqk",
                     "fx", "fl", "foxcum", "scores", "scores_read", "nmax", "probs", "pnorm", "pturned", "pt",
                     "pv", "outh", "o", "gu_sq", "gu_t", "gu_e", "gu", "lnv", "lny", "gv", "gmix", "dout_sq",
                     "cmean", "cvar_sq", "cexp", "cy", "dout", "craw",
                     "sq", "lam", "sigm", "silu", "hz", "hz1", "hz2", "hz3", "hz4", "ld", "le", "lx", "lmm", "sunk", "esink",
                     "hpv", "hsq", "gates", "branch", "mixed", "mixh", "hcum")
        s = {n: sem(n) for n in mix_names}
        y_out, y_stored = sem("y_out"), sem("y_stored")

        def cols8(w, l, at, n=256):
            v = w.rearrange("l (c p) n -> l p c n", p=P)
            return v[bass.ds(l, 1), :, :, bass.ds(at, n)].rearrange("l p c n -> p (l c) n")

        def rows2(w, l, g, n):
            v = w.rearrange("l (g f p) n -> (l g) p f n", f=2, p=P)
            return v[bass.ds(l * n + g, 1)].rearrange("l p f n -> p (l f) n")

        def cols4(w, l, at):
            v = w.rearrange("l (c p) n -> l p c n", p=P)
            return v[bass.ds(l, 1), :, :, bass.ds(at, 512)].rearrange("l p c n -> p (l c) n")

        unit8 = [r[:, :].rearrange("p (c n) -> p c n", c=8) for r in (raw[:, i, :] for i in range(3))]

        def as8(t, j):
            return t[:, j, :].rearrange("p (c n) -> p c n", c=8)

        def as2(t, j):
            return t[:, j, :].rearrange("p (f n) -> p f n", f=2)

        def as4(t, j):
            return t[:, j, :].rearrange("p (c n) -> p c n", c=4)

        class Layer:

            def __init__(self, blk, l):
                self.b, self.l = blk, l
                before = LAYERS * NU[0] if blk else 0
                self.u0, self.nu = before, NU[blk]

            def unit(self, k, i=0):
                return self.u0 + self.l * self.nu + k + 3 * i

            def turn(self, k, i=0):
                return self.u0 // 3 + self.l * (self.nu // 3) + k // 3 + i

            def sub(self, j):
                n = [len(p) for p in PARTS]
                return (LAYERS * n[0] if self.b else 0) + self.l * n[self.b] + j

            def ffn(self, j):
                n = [sum(q == "ffn" for q in p) for p in PARTS]
                at = sum(q == "ffn" for q in PARTS[self.b][:j])
                return (LAYERS * n[0] if self.b else 0) + self.l * n[self.b] + at

            def event(self, e):
                return (LAYERS * EVENTS[0] if self.b else 0) + self.l * EVENTS[self.b] + e

            def nth(self, per, k):
                return self.l * per + k

        def parts(blk):
            k = e = 0
            for j, kind in enumerate(PARTS[blk]):
                yield kind, j, k, e
                k += UNITS[(kind, blk)]
                e += EVENTS_OF[(kind, blk)]

        def bank_done(eng, L, kind, j, k, b):
            if kind == "mix":
                eng.wait_ge(unit_used, L.unit(k - 3 + b) + 4)
            elif b < 3:
                eng.wait_ge(acc_done, 3 * L.ffn(j) + b + 1)
            else:
                eng.wait_ge(unit_used, L.unit(k) + 4)

        def unit_form(L, k):
            return "F" if L.b == 0 and "mix" in PARTS[0] and k == FFN_UNITS + 4 else "T"

        SUBS = LAYERS * (len(PARTS[0]) + len(PARTS[1]))

        def NSQ(L, j, e, post=False):
            more = 8 * (L.l * len(PARTS[1]) + j) + (8 if post else 0) if L.b else 0
            return 8 * L.sub(j) + more

        def rows(a, pattern):
            return a.rearrange(pattern, p=P)

        stage_rows = [
            (stage[0:72, 0, :], rows(ada_b[0], "(a p) -> a p")),
            (stage[72:120, 0, :], rows(norm_g, "l j (m p) -> (l j m) p")),
            (stage[120:128, 0, :], rows(c, "b (m p) -> (b m) p")),
            (stage[0:72, 1, :], rows(ada_b[1], "(a p) -> a p")),
            (stage[72:76, 1, :], rows(conv_b, "l (c p) -> (l c) p")),
            (stage[76:80, 1, :], rows(conv_norm_g, "l (c p) -> (l c) p")),
            (stage[80:84, 1, :], rows(conv_norm_b, "l (c p) -> (l c) p")),
            (stage[84:92, 1, :], rows(hgrn_lower_bounds_2, "l (h p) -> (l h) p")),
            (stage[92:94, 1, :], hgrn_head_gain_2),
            (stage[0:96, 2, :], rows(norm_gains_2, "l r (m p) -> (l r m) p")),
            (stage[0:124, 3, :], rows(conv_w, "l j (c p) -> (l j c) p"))]
        STAGES, STAGE_ROWS = len(stage_rows), (128, 94, 96, 124)

        def everywhere(a, n=P):
            return a.partition_broadcast(n)

        smalls = [(foxg[64 * r:64 * r + 64, :], fox_qk_g.rearrange("l t d -> d (l t)")) for r in range(2)]
        smalls += [(diffg[32 * r:32 * r + 32, :], diff_qk_g.rearrange("l t d -> d (l t)")) for r in range(4)]
        smalls += [(dog[64 * r:64 * r + 64, :], diff_out_g.rearrange("l d -> d l")) for r in range(2)]
        smalls += [(fb[0:4, :], fox_fb.rearrange("l h -> h l")),
                   (sinkb[:, :], everywhere(attn_sinks_2.rearrange("l h -> (l h)"))),
                   (lraw[:, :, :], everywhere(diff_lambda.rearrange("l a d -> (l a) d"))),
                   (ngb[:, 0], everywhere(gmlp_norm_g)), (ngb[:, 1], everywhere(gmlp_norm_b)),
                   (wsn[:, :, :], gmlp_ws.rearrange("l h t s -> t (l h) s"))]
        for r in range(2):
            smalls += [(bsb[64 * r:64 * r + 64, l], everywhere(gmlp_bs[l].rearrange("(c r) t -> r c t", r=2)[r], 64))
                       for l in range(LAYERS)]
        SMALLS = len(smalls)

        ZU1 = [("ca", 768, "T"), ("cg", 1024, "T"), ("fq", 1792, "T"), ("fk", 2048, "T"), ("f", 2560, "F"),
               ("fv", 2304, "N"), ("dq", 0, "T"), ("dk", 256, "T"), ("dv", 512, "N"), ("gu", 1280, "T"),
               ("gv", 1536, "N")]
        zi = {name: i for i, (name, _, _) in enumerate(ZU1)}
        ZU2 = ([("hq", 0, "T"), ("hq", 256, "T"), ("hg", 1536, "T"), ("hg", 1792, "T"), ("hf", 512, "T"),
                ("hf", 768, "T"), ("hi", 1024, "N"), ("hi", 1280, "N"), ("aq", 2048, "Q"), ("aq", 2176, "Q"),
                ("akv", 2560, "K")] + [("g", 2816 + 256 * i, "T") for i in range(8)])
        PLAN1 = {1: ["convin"], 3: ["foxqk"], 4: ["foxf"], 5: ["foxs"], 6: ["foxt"], 7: ["diffqk"],
                 8: ["diffs0"], 9: ["diffs1", "gelu_u"],
                 10: ["foxout", "difft", "gelu_v", "gmlp", "diffout", "convout"]}
        PLAN2 = {3: ["silu"], 5: ["hprep"], 6: ["lev0"], 7: ["lev1"], 8: ["lev2"], 9: ["lev3"], 10: ["lev4"],
                 11: ["lev5"], 12: ["lev6"], 13: ["lev7", "lev8"], 14: ["hlast"], 15: ["att0"], 16: ["attt0"],
                 17: ["att1"], 18: ["attt1", "hout", "attout", "gates"]}
        HEAD1 = {"foxs": 0, "diffs0": 1, "diffs1": 2}

        block = ctx.enter_context(nc.Block())

        @block.sync
        def _(sp):
            sp.dma_start(sq8[:, :].rearrange("p (a d) -> p a d", a=2),
                         x.rearrange("b (a p) d -> p (b a) d", p=P)).then_inc(x_loaded, 16)
            ada0 = ada_w[0].rearrange("(c p) n -> c p n", p=P)
            for k in range(KC):
                if k >= 3:
                    sp.wait_ge(ada0_used, k - 2)
                sp.dma_start(adaf[:, k % 3], ada0[k, :, 0:3072]).then_inc(ada0_loaded[k % 3], 16)

            def load(L, k, pieces, i=0):
                sp.wait_ge(lo_done, L.unit(k, i) + 1)
                sp.sem_inc(sp_waited, 1)
                for dst, src in pieces:
                    sp.dma_start(dst, src).then_inc(raw_loaded[k % 3], LOADED // len(pieces))

            def whole(form, k, src):
                return [(form(raw, k % 3), src)]

            for blk in range(2):
                if not PARTS[blk]:
                    continue
                with sp.Fori(0, LAYERS) as l:
                    L = Layer(blk, l)
                    for kind, j, k0, _ in parts(blk):
                        if kind == "ffn":
                            if blk == 0:
                                wi, wd = ((ffn1_w_in, ffn1_w_out), (ffn2_w_in, ffn2_w_out))[j // 2]
                                wg, wu, ug = wi, wi, DFF
                            else:
                                wg, wu, wd = ((w_ffn1_gate_2, w_ffn1_up_2, w_ffn1_down_2),
                                              (w_ffn2_gate_2, w_ffn2_up_2, w_ffn2_down_2))[j // 2]
                                ug = 0
                            load(L, k0, whole(as8, k0, cols8(wg, l, 0)))
                            load(L, k0 + 1, whole(as8, k0 + 1, cols8(wu, l, ug)))

                            def group(i, ada=False):
                                load(L, k0 + 2, whole(as8, k0 + 2, cols8(wg, l, i * 256 + 256)), i)
                                load(L, k0 + 3, whole(as8, k0 + 3, cols8(wu, l, i * 256 + (ug + 256))), i)
                                load(L, k0 + 4, whole(as2, k0 + 4, rows2(wd, l, i, GROUPS)), i)
                                if ada:
                                    sp.wait_ge(ada1_used, l * KC + i + 1)
                                    sp.sem_inc(sp_waited, 1)
                                    src = ada_w.rearrange("l (c p) n -> (l c) p n", p=P)[
                                        bass.ds(l * KC + i, 1), :, 3072:6144].rearrange("c p n -> p (c n)")
                                    sp.dma_start(adam, src).then_inc(ada1_loaded, 16)

                            mixers = blk == 0 and j == 0 and "mix" in PARTS[0]
                            if mixers:
                                with sp.Fori(0, KC) as i:
                                    group(i, True)
                            with sp.Fori(KC if mixers else 0, GROUPS - 1) as i:
                                group(i)
                            load(L, k0 + FFN_UNITS - 1, whole(as2, k0 + FFN_UNITS - 1, rows2(wd, l, GROUPS - 1, GROUPS)))
                        elif blk == 0:
                            for n, (name, col, form) in enumerate(ZU1):
                                k = k0 + n
                                if form == "F":
                                    with nc.allow_non_contiguous_dma(reason="four columns of forget logits"):
                                        load(L, k, [(as8(raw, k % 3)[:, :, 0:4], cols8(w_in, l, col, 4))])
                                else:
                                    load(L, k, whole(as8, k, cols8(w_in, l, col)))
                            for n in range(4):
                                load(L, k0 + 11 + n, whole(as8, k0 + 11 + n, cols8(w_out, l, 256 * n)))
                        else:
                            for n, (name, col, form) in enumerate(ZU2):
                                k = k0 + n
                                if form == "Q":
                                    v = w_in_2.rearrange("l (c p) n -> l p c n", p=P)
                                    d = as8(raw, k % 3).rearrange("p c (h g d) -> p c h g d", h=2, g=2)
                                    load(L, k, [(d[:, :, h, g], v[bass.ds(l, 1), :, :, bass.ds(
                                        col + 64 * h + 256 * g, 64)].rearrange("l p c n -> p (l c) n"))
                                        for g in range(2) for h in range(2)])
                                else:
                                    load(L, k, whole(as8, k, cols8(w_in_2, l, col)))
                            for n in range(2):
                                load(L, k0 + 19 + n, whole(as4, k0 + 19 + n, cols4(w_branch_hgrn_2, l, 512 * n)))
                            for n in range(2):
                                k = k0 + 21 + n
                                v = w_branch_attn_2.rearrange("l (g c d) n -> l g d c n", g=2, c=4)
                                load(L, k, [(as4(raw, k % 3)[64 * g:64 * g + 64],
                                             v[bass.ds(l, 1), g, :, :, 512 * n:512 * n + 512]
                                             .rearrange("l d c n -> d (l c) n")) for g in range(2)])
                            for n in range(4):
                                load(L, k0 + 23 + n, whole(as8, k0 + 23 + n, cols8(w_out_2, l, 256 * n)))
            sp.wait_ge(y_out, 1)
            sp.dma_start(out.rearrange("b (a p) d -> p (b a) d", p=P),
                         sq8[:, :].rearrange("p (a d) -> p a d", a=2)).then_inc(y_stored, 16)
            sp.wait_ge(y_stored, 16)

        def seq(L, per, k, kind="mix"):
            before = LAYERS * per[0] if L.b and kind in PARTS[0] else 0
            return before + L.l * per[L.b] + k

        NZ = (len(ZU1), len(ZU2))
        ROUNDS, TURNS, OUTS, SQS = (3, 2), (2, 2), (4, 2), (4, 1)
        zbank = [ps[:, i % 2, :] for i in range(2)]
        sc0 = ps[:, 2, :].rearrange("p (h k) -> p h k", h=4)
        sc1 = ps[:, 3:5, :].rearrange("p b n -> p (b n)").rearrange("p (h k) -> p h k", h=4)
        turned = ps[:, 2:5, :].rearrange("p b n -> p (b n)")
        stat2 = ps[:, 6:8, :].rearrange("p b n -> p (b n)")
        hstat = ps[:, 2:4, :].rearrange("p b n -> p (b n)")
        lbank = [ps[:, 2:4, :].rearrange("p b n -> p (b n)"), ps[:, 4:6, :].rearrange("p b n -> p (b n)")]
        u8h = [u8[:, 0:1024], u8[:, 1024:2048]]
        sq8h = [sq8[:, 0:1024], sq8[:, 1024:2048]]
        s0f = S0[:, :, :].rearrange("p h k -> p (h k)")
        s1f = u8[:, 0:1536]
        br_bank = [ps[:, b:b + 2, :].rearrange("p b n -> p (b n)") for b in (2, 4, 0, 6)]
        zt = {n: Z[:, i, :] for n, i in zi.items()}
        z2dst = ([HQ, HQ, HG, HG, HF, HF])

        def z_dest(blk, i):
            if blk == 0:
                return Z[:, i, :]
            if i < 6:
                return arena[:, 512 * i:512 * i + 512]
            if i < 8:
                return HV[:, :, 256 * (i - 6):256 * (i - 6) + 256]
            if i < 10:
                return AQ[:, 2 * (i - 8):2 * (i - 8) + 2, :]
            if i == 10:
                return arena[:, 7168:7680]
            return GA[:, 2 * (i - 11):2 * (i - 11) + 2, :]

        @block.tensor
        def _(pe):
            def mm3(o, wh, wl, ah, al, start, stop, **kw):
                pe.matmul(o, wh, al, start=start, stop=False, **kw)
                pe.matmul(o, wl, ah, start=False, stop=False, **kw)
                return pe.matmul(o, wh, ah, start=False, stop=stop, **kw)

            def split_ready(L, k, i=0):
                pe.wait_ge(lo_done, L.unit(k, i) + 4)

            pe.drain().then_inc(unit_used, 3)
            pe.wait_ge(consts_ready, 1)
            pe.wait_ge(stage_loaded, STAGES * 16)
            for t, n in enumerate(STAGE_ROWS):
                ins = pe.transpose(ps[:, 7, t * P:t * P + n], stage[0:n, t, :], ident[0:n, 0:n])
            ins.then_inc(stage_turned, 1)
            pe.wait_ge(x_loaded, 16)
            for m in range(KC):
                for a in range(2):
                    ins = pe.transpose(ps[:, m // 2, (m % 2) * 256 + a * P:(m % 2) * 256 + a * P + P],
                                       sq8[:, a * D + m * P:a * D + m * P + P], ident[:, :])
                if m % 2:
                    ins.then_inc(x_turned, 1)
            pe.wait_ge(smalls_loaded, SMALLS * 16)
            for i in range(8):
                ins = pe.transpose(ps[:, 4 + i // 4, (i % 4) * P:(i % 4) * P + P], wsn[:, i, :], ident[:, :])
                if i % 4 == 3:
                    ins.then_inc(ws_turned, 1)
            pe.wait_ge(dconsts_ready, 1)

            def modulation(L, j):
                pe.wait_ge(ada_ready[j], L.l + 1)
                for t in range(24):
                    ins = pe.matmul(ps[:, 7, t:t + 1], acc[:, j % 2, t * P:t * P + P], ones_col[:, 0:1],
                                    start=True, stop=True)
                ins.then_inc(mod_summed, 1)

            def norm(L, j, e):
                if L.b == 0 and j == 0:
                    modulation(L, j)
                for m in range(KC):
                    pe.wait_ge(nsq_ready, NSQ(L, j, e) + (m + 1))
                    ins = pe.matmul(ps[:, STAT, 0:S], ones_d[:, :], sq8[:, m * S:m * S + S],
                                    start=(m == 0), stop=(m == KC - 1))
                ins.then_inc(ms_ready, 1)

            def post_norm(L, j, e):
                for m in range(KC):
                    if m % 2 == 0:
                        pe.wait_ge(nsq_ready, NSQ(L, j, e, post=True) + 2 * (m // 2 + 1))
                    ins = pe.matmul(ps[:, STAT, 0:S], ones_d[:, :], sq8[:, m * S:m * S + S],
                                    start=(m == 0), stop=(m == KC - 1))
                ins.then_inc(ms_ready, 1)

            def ffn(L, st, j, k0):
                n, g0 = L.sub(j), L.ffn(j) * GROUPS
                for b in range(4):
                    pe.matmul(ps[:, ACC + b, :], zerow[:, 0:P], zerow[:, :], start=True, stop=True,
                              skip_group_check=True)

                def half(k, bank, i=0, first=False):
                    split_ready(L, k, i)
                    wh, wl = as8(whi, k % 3), as8(wlo, k % 3)
                    for f in range(2):
                        for kc in range(KC):
                            if first and f == 0:
                                pe.wait_ge(x_ready, 8 * n + kc + 1)
                            ins = mm3(ps[:, bank, f * S:f * S + S], wh[:, kc, f * P:f * P + P],
                                      wl[:, kc, f * P:f * P + P], xh[:, kc, :], xl[:, kc, :],
                                      start=(kc == 0), stop=(kc == KC - 1))
                    ins.then_inc(unit_used, 1)

                def down(k, g, i=0, last=False):
                    split_ready(L, k, i)
                    pe.wait_ge(hid_ready, g0 + g + 1)
                    wh, wl = as2(whi, k % 3), as2(wlo, k % 3)
                    for f, m in ([(f, m) for m in range(KC) for f in range(2)] if last else
                                 [(f, m) for f in range(2) for m in range(KC)]):
                        ins = mm3(ps[:, ACC + m // 2, (m % 2) * S:(m % 2) * S + S],
                                  wh[:, f, m * P:m * P + P], wl[:, f, m * P:m * P + P],
                                  hidh[:, f * S:f * S + S], hidl[:, f * S:f * S + S],
                                  start=False, stop=False, skip_group_check=True)
                        if last and f == 1 and m in (1, 3, 5):
                            ins.then_inc(acc_done, 1)
                    ins.then_inc(unit_used, 1)

                half(k0, G_BANK, first=True)
                half(k0 + 1, U_BANK)
                with pe.Fori(0, GROUPS - 1) as i:
                    pe.wait_ge(h32_ready, g0 + i + 1)
                    half(k0 + 2, G_BANK, i)
                    half(k0 + 3, U_BANK, i)
                    down(k0 + 4, i, i)
                if L.b == 0 and j == 0:
                    modulation(L, 1)
                down(k0 + FFN_UNITS - 1, GROUPS - 1, last=True)

            def scores(L, st, q, k, base, width, gates=False):
                out_of = [lambda h: sc0[:, h, :], lambda h: sc1[:, h, :]]
                if gates:
                    for b in range(3):
                        ins = pe.matmul(ps[:, 2 + b, :], zerow[:, 0:P], zerow[:, :], start=True, stop=True,
                                        skip_group_check=True)
                    st(ins)
                last = None
                for r0 in sorted({base(h)[0] for h in range(4)}):
                    if last is not None:
                        st(last)
                    for h in range(4):
                        if base(h)[0] != r0:
                            continue
                        ch = base(h)[1]
                        for qb in range(2):
                            last = pe.matmul(out_of[qb](h), q[r0:r0 + width, ch, qb * P:qb * P + P],
                                             k(r0, width, ch)[:, 0:P * (qb + 1)], start=not gates, stop=True,
                                             skip_group_check=gates)
                if gates:
                    st(last)
                    for h in range(4):
                        for qb in range(2):
                            o, keys = out_of[qb](h), P * (qb + 1)
                            pe.matmul(o, gcum[0:4, 0, qb * P:qb * P + P], sel[0:4, h, 0:keys], start=False,
                                      stop=True, skip_group_check=True)
                            last = pe.matmul(o, sel[0:4, h, 0:P], gcum[0:4, 1, 0:keys], start=False, stop=True,
                                             skip_group_check=True)
                last.then_inc(s["scores"], 1)

            def turn(L, t, probs):
                pe.wait_ge(s["pnorm"], seq(L, TURNS, t + 1))
                for h in range(4):
                    for b in range(3):
                        ins = pe.transpose(turned[:, (3 * h + b) * P:(3 * h + b + 1) * P],
                                           probs[:, h, b * P:b * P + P], ident[:, :])
                ins.then_inc(s["pturned"], 1)

            def values(L, t, v, pt, place):
                pe.wait_ge(s["pt"], seq(L, TURNS, t + 1))
                for h in range(4):
                    o = place(h)
                    pe.matmul(o, v(h, 0), pt[:, h * 384:h * 384 + 256], start=True, stop=False)
                    ins = pe.matmul(o[:, P:S], v(h, 1), pt[:, h * 384 + 256:h * 384 + 384], start=False, stop=True)
                ins.then_inc(s["pv"], 1)

            def head_stat(L, e, q, m, src, dst):
                pe.wait_ge(s["sq"], seq(L, SQS, q + 1))
                for b in range(len(dst)):
                    ins = pe.matmul(dst[b], m[:, :], src[:, b * 512:b * 512 + 512], start=True, stop=True)
                ins.then_inc(ms_ready, 1)

            def stage1(L, st, name):
                if name == "foxqk":
                    head_stat(L, 2, 0, blk64, sq8, [ps[:, 6, :], ps[:, 7, :]])
                elif name == "diffqk":
                    head_stat(L, 3, 1, blk32, sq8, [ps[:, 6, :], ps[:, 7, :]])
                elif name == "foxs":
                    pe.wait_ge(s["foxqk"], L.l + 1)
                    pe.wait_ge(s["foxcum"], L.l + 1)
                    fq = zt["fq"].rearrange("p (c t) -> p c t", c=2)
                    fk = zt["fk"].rearrange("p (c t) -> p c t", c=2)
                    scores(L, st, fq, lambda r, w, c: fk[r:r + w, c, :], lambda h: (64 * (h % 2), h // 2), 64, True)
                elif name in ("diffs0", "diffs1"):
                    c = int(name[-1])
                    if c == 0:
                        pe.wait_ge(s["diffqk"], L.l + 1)
                        pe.wait_ge(s["pt"], seq(L, TURNS, 1))
                    else:
                        pe.wait_ge(s["scores_read"], seq(L, ROUNDS, 2))
                    dq = zt["dq"].rearrange("p (c t) -> p c t", c=2)
                    dk = zt["dk"].rearrange("p (c t) -> p c t", c=2)
                    scores(L, st, dq, lambda r, w, ch: dk[r:r + w, ch, :],
                           lambda h: (64 * (h % 2) + 32 * c, h // 2), 32)
                elif name in ("foxt", "difft"):
                    t = 0 if name == "foxt" else 1
                    turn(L, t, S0)
                    v = zt["fv" if t == 0 else "dv"].rearrange("p (b e) -> p b e", b=2)
                    if t == 1:
                        pe.wait_ge(s["o"], seq(L, OUTS, 1))
                    values(L, t, lambda h, b: v[:, b, 64 * h:64 * h + 64], PT1,
                           lambda h: ps[64 * (h % 2):64 * (h % 2) + 64, PVB, (h // 2) * S:(h // 2) * S + S])
                elif name == "gmlp":
                    pe.wait_ge(s["gv"], L.l + 1)
                    v = zt["gv"].rearrange("p (b e) -> p b e", b=2)
                    for h in range(4):
                        for b in range(2):
                            at = (h // 2) * S + b * P
                            ins = pe.matmul(ps[64 * (h % 2):64 * (h % 2) + 64, 7, at:at + P],
                                            v[:, b, 64 * h:64 * h + 64],
                                            zt["fq"][:, h * P:h * P + P],
                                            start=True, stop=True)
                    ins.then_inc(s["gmix"], 1)
                elif name == "diffout":
                    head_stat(L, 4, 2, blk64, u8[:, 1536:2048], [ps[:, 6, :]])
                elif name == "convout":
                    cx = zt["ca"].rearrange("p (c t) -> p c t", c=2)
                    pe.wait_ge(s["conv_done"], L.l + 1)
                    for ch in range(2):
                        ins = pe.matmul(ps[:, 2, 0:S], ones_d[:, :], cx[:, ch, :], start=(ch == 0), stop=(ch == 1))
                    ins.then_inc(s["cmean"], 1)
                    pe.wait_ge(s["sq"], seq(L, SQS, 4))
                    csq = zt["cg"].rearrange("p (c t) -> p c t", c=2)
                    for ch in range(2):
                        ins = pe.matmul(ps[:, 3, 0:S], ones_d[:, :], csq[:, ch, :], start=(ch == 0), stop=(ch == 1))
                    ins.then_inc(ms_ready, 1)

            def stage2(L, st, name):
                if name.startswith("lev"):
                    n = int(name[3:])
                    if n == 0:
                        pe.wait_ge(s["hcum"], L.l + 1)
                        left, right = HK[:, :, :], HQ[:, :, :]
                        left = left.rearrange("p h t -> p (h t)")
                        right = right.rearrange("p h t -> p (h t)")
                    else:
                        pe.wait_ge(s["lx"], L.l * 8 + n)
                        left = right = sq8h[n % 2]
                    if n < 8:
                        for b in range(8):
                            ins = pe.matmul(lbank[n % 2][:, b * P:b * P + P], left[:, b * P:b * P + P],
                                            right[:, b * P:b * P + P], start=True, stop=True)
                    else:
                        for h in range(4):
                            ins = pe.matmul(lbank[n % 2][:, h * P:h * P + P], left[:, h * S:h * S + P],
                                            right[:, h * S + P:h * S + S], start=True, stop=True)
                    ins.then_inc(s["lmm"], 1)
                elif name == "hlast":
                    pe.wait_ge(s["hz"], L.l + 1)
                    for h in range(4):
                        o = stat2[:, h * S:h * S + S]
                        v0, v1 = HV[:, 0, h * P:h * P + P], HV[:, 1, h * P:h * P + P]
                        pe.matmul(o[:, 0:P], v0, AT[:, 2 * h, :], start=True, stop=True)
                        pe.matmul(o[:, P:S], v0, AT[:, 8 + h, :], start=True, stop=False)
                        ins = pe.matmul(o[:, P:S], v1, AT[:, 2 * h + 1, :], start=False, stop=True)
                    ins.then_inc(s["hpv"], 1)
                elif name in ("att0", "att1"):
                    g = int(name[-1])
                    if g:
                        pe.wait_ge(s["pt"], seq(L, TURNS, 1))
                    scores(L, st, AQ, lambda r, w, c: AK[r:r + w, :], lambda h: (64 * g, h), 64)
                elif name in ("attt0", "attt1"):
                    g = int(name[-1])
                    turn(L, g, S1)
                    if g == 0:
                        pe.wait_ge(s["hsq"], L.l + 1)
                    values(L, g, lambda h, b: AV[:, b, 64 * g:64 * g + 64], PT1,
                           lambda h: stat2[64 * g:64 * g + 64, h * S:h * S + S])
                elif name == "hout":
                    pe.wait_ge(s["sq"], seq(L, SQS, 1))
                    for b in range(2):
                        ins = pe.matmul(hstat[:, b * 512:b * 512 + 512], ones_128[:, :],
                                        sq8[:, b * 512:b * 512 + 512], start=True, stop=True)
                    ins.then_inc(ms_ready, 1)

            def mix(L, st, j, k0):
                units = ZU2 if L.b else ZU1
                plan, stage_of = (PLAN2, stage2) if L.b else (PLAN1, stage1)
                for i, (_, _, form) in enumerate(units):
                    k = k0 + i
                    split_ready(L, k)
                    if i >= 2:
                        pe.wait_ge(z_copied[L.b], L.l * NZ[L.b] + i - 1)
                    wh, wl = as8(whi, k % 3), as8(wlo, k % 3)
                    for f in range(1 if form == "F" else 2):
                        o = ps[:, i % 2, f * S:f * S + S]
                        natural = form == "N" or (form == "K" and f == 1)
                        if form == "K" and f == 1:
                            for a in range(2):
                                for kc in range(KC):
                                    ins = mm3(o[:, a * P:a * P + P], xh[:, kc, a * P:a * P + P],
                                              xl[:, kc, a * P:a * P + P], wh[:, kc, P:2 * P], wl[:, kc, P:2 * P],
                                              start=(kc == 0), stop=(kc == KC - 1))
                        elif natural:
                            for kc in range(KC):
                                ins = mm3(o, xh[:, kc, f * P:f * P + P], xl[:, kc, f * P:f * P + P],
                                          wh[:, kc, :], wl[:, kc, :], start=(kc == 0), stop=(kc == KC - 1))
                        else:
                            for kc in range(KC):
                                if i == 0 and f == 0:
                                    pe.wait_ge(x_ready, 8 * L.sub(j) + kc + 1)
                                ins = mm3(o, wh[:, kc, f * P:f * P + P], wl[:, kc, f * P:f * P + P],
                                          xh[:, kc, :], xl[:, kc, :], start=(kc == 0), stop=(kc == KC - 1))
                    ins.then_inc(unit_used, 1)
                    for name in plan.get(i - 1, []):
                        stage_of(L, st, name)
                for name in plan.get(len(units) - 1, []):
                    stage_of(L, st, name)
                nb = 0
                if L.b:
                    for n in range(4):
                        k = k0 + 19 + n
                        split_ready(L, k)
                        if n == 0:
                            pe.wait_ge(s["o"], seq(L, OUTS, 1))
                        if n == 2:
                            pe.wait_ge(s["o"], seq(L, OUTS, 2))
                        wh, wl = as4(whi, k % 3), as4(wlo, k % 3)
                        for m in range(4):
                            for kc in range(4):
                                x0 = 4 * (n // 2) + kc
                                ins = mm3(br_bank[n][:, m * S:m * S + S], wh[:, kc, m * P:m * P + P],
                                          wl[:, kc, m * P:m * P + P], xh[:, x0, :], xl[:, x0, :],
                                          start=(kc == 0), stop=(kc == 3))
                        ins.then_inc(unit_used, 1)
                    pe.wait_ge(s["mixed"], 8 * L.l + 8)
                    nb = 4
                else:
                    pe.wait_ge(s["o"], seq(L, OUTS, 4))
                for n in range(4):
                    if L.b == 0 and n == 3:
                        modulation(L, 2)
                    k = k0 + len(units) + nb + n
                    split_ready(L, k)
                    wh, wl = as8(whi, k % 3), as8(wlo, k % 3)
                    for f in range(2):
                        for kc in range(KC):
                            ins = mm3(ps[:, ACC + n, f * S:f * S + S], wh[:, kc, f * P:f * P + P],
                                      wl[:, kc, f * P:f * P + P], xh[:, kc, :], xl[:, kc, :],
                                      start=(kc == 0), stop=(kc == KC - 1))
                    ins.then_inc(unit_used, 1)

            for blk in range(2):
                if not PARTS[blk]:
                    continue
                with pe.Fori(0, LAYERS) as l:
                    L = Layer(blk, l)
                    st = Steps(pe, pe_step[blk], l, PE_STEPS[blk])
                    for kind, j, k0, e in parts(blk):
                        norm(L, j, e)
                        (ffn if kind == "ffn" else mix)(L, st, j, k0)
                        if blk:
                            post_norm(L, j, e)
                    assert st.k == PE_STEPS[blk], ("PE_STEPS", blk, st.k)
            pe.wait_ge(h_ready, 8 * SUBS + 8)
            for a in range(2):
                for m in range(KC):
                    ins = pe.transpose(ps[:, 2 * a + m // 4, (m % 4) * P:(m % 4) * P + P],
                                       hT[:, m, a * P:a * P + P], ident[:, :])
            ins.then_inc(x_turned, 1)

        @block.scalar
        def _(act):
            for dst, src in stage_rows:
                act.dma_start(dst, src).then_inc(stage_loaded, 16)
            with nc.allow_non_contiguous_dma(reason="a few hundred parameters, an element a partition"):
                for dst, src in smalls:
                    act.dma_start(dst, src).then_inc(smalls_loaded, 16)
            act.wait_ge(prm_ready, 1)
            act.activation(condT[:, 0, :], prm[:, 120:128], ACT.Exp, scale=-1.0).then_inc(act_setup, 1)
            act.wait_ge(s["lam"], 1)
            act.activation(lamb[:, 4:8], lamb[:, 0:4], ACT.Exp).then_inc(act_setup, 1)
            act.wait_ge(s["lam"], 2)
            act.activation(lbt[:, 2:4, :], lbt[:, 0:2, :], ACT.Exp).then_inc(act_setup, 1)
            act.wait_ge(s["lam"], 3)
            act.activation(lbt[:, 5, :], lbt[:, 4, :], ACT.Ln).then_inc(act_setup, 1)

            def hi(L, k, i=0):
                act.wait_ge(raw_loaded[k % 3], LOADED * L.turn(k, i) + LOADED)
                act.wait_ge(unit_used, L.unit(k, i) + 1)
                if L.b == 0 and unit_form(L, k) == "F":
                    act.activation(as8(whi, k % 3)[:, :, 0:4], as8(raw, k % 3)[:, :, 0:4],
                                   ACT.Copy).then_inc(hi_done, 1)
                else:
                    act.activation(whi[:, k % 3, :], raw[:, k % 3, :], ACT.Copy).then_inc(hi_done, 1)

            def used(L, k, i=0):
                act.wait_ge(unit_used, L.unit(k, i) + 4)

            def rs(st, e, y, ms):
                act.wait_ge(ms_ready, e + 1)
                st(act.activation(y, ms, ACT.Ln, bias=epsc[:, 0:1]))
                act.activation(y, y, ACT.Exp, scale=-0.5).then_inc(y_ready, 1)

            def norm(L, st, j, e, k0):
                n = L.sub(j)
                if j == 0:
                    hi(L, k0)
                for m in range(KC):
                    act.wait_ge(h_ready, 8 * n + (m + 1))
                    act.activation(sq8[:, m * S:m * S + S], hT[:, m, :], ACT.Square).then_inc(nsq_ready, 1)
                rs(st, L.event(e), nrm[:, 0, :], ps[:, STAT, 0:S])
                for m in range(KC):
                    act.wait_ge(u_ready, 8 * n + (m + 1))
                    act.activation(xh[:, m, :], u8[:, m * S:m * S + S], ACT.Identity,
                                   bias=gB[:, m:m + 1]).then_inc(xh_ready, 1)
                hi(L, k0 + 1)

            def post_norm(L, st, kind, j, e, klast):
                for b in range(4):
                    bank_done(act, L, kind, j, klast, b)
                    act.activation(sq8[:, b * 512:b * 512 + 512], ps[:, ACC + b, :],
                                   ACT.Square).then_inc(nsq_ready, 2)
                rs(st, L.event(e), nrm[:, 0, :], ps[:, STAT, 0:S])

            def ffn(L, st, j, k0):
                g0 = L.ffn(j) * GROUPS

                def sigmoid(k, i=0):
                    used(L, k, i)
                    act.activation(sq8[:, 0:512], ps[:, G_BANK, :], ACT.Sigmoid).then_inc(sig_ready, 1)

                def upper(g):
                    act.wait_ge(h32_ready, g0 + g + 1)
                    act.activation(hidh[:, :], u8[:, 0:512], ACT.Copy).then_inc(hidh_ready, 1)

                hi(L, k0 + 2)
                sigmoid(k0)
                hi(L, k0 + 3)
                upper(0)
                with act.Fori(0, GROUPS - 2) as i:
                    hi(L, k0 + 4, i)
                    sigmoid(k0 + 2, i)
                    hi(L, k0 + 5, i)
                    hi(L, k0 + 6, i)
                    used(L, k0 + 4, i)
                    upper(i + 1)
                k = k0 + 3 * (GROUPS - 2)
                hi(L, k + 4)
                sigmoid(k + 2)
                hi(L, k + 5)
                used(L, k + 4)
                upper(GROUPS - 1)

            def copied(L, i):
                act.wait_ge(z_copied[L.b], L.l * NZ[L.b] + i + 1)

            def softmax(L, a, tile, sink=False):
                act.wait_ge(s["nmax"], seq(L, ROUNDS, a + 1))
                for qb in range(2):
                    for h in range(4):
                        seg = tile[:, h, P:3 * P] if qb else tile[:, h, 0:P]
                        c = 4 * qb + h
                        ins = act.activation(seg, seg, ACT.Exp, bias=nmx[:, c:c + 1], accum_out=ssum[:, c:c + 1])
                if sink:
                    ins = act.activation(sinke[:, :], sinke[:, :], ACT.Exp)
                ins.then_inc(s["probs"], 1)

            def turned_out(L, t):
                act.wait_ge(s["pturned"], seq(L, TURNS, t + 1))
                if t:
                    act.wait_ge(s["pv"], seq(L, TURNS, 1))
                act.activation(PT1, turned, ACT.Copy).then_inc(s["pt"], 1)

            def xo(a, b):
                return xh[:, a:b, :].rearrange("p c t -> p (c t)")

            def stage1(L, st, k0, name):
                l = L.l
                if name == "convin":
                    copied(L, zi["cg"])
                    act.activation(u8[:, 0:512], zt["cg"], ACT.Exp, scale=-1.0).then_inc(s["convexp"], 1)
                elif name in ("foxqk", "diffqk"):
                    q = 0 if name == "foxqk" else 1
                    a = zi["fq" if q == 0 else "dq"]
                    copied(L, a + 1)
                    if q:
                        act.wait_ge(s["pv"], seq(L, TURNS, 1))
                    act.activation(sq8h[0], Z[:, a:a + 2, :].rearrange("p a n -> p (a n)"),
                                   ACT.Square).then_inc(s["sq"], 1)
                    rs(st, L.event(2 + q), sq8h[1], stat2)
                elif name == "foxf":
                    act.wait_ge(s["fx"], l + 1)
                    f, w = zt["f"][0:4, 0:S], zt["f"][0:4, S:2 * S]
                    st(act.activation(w, f, ACT.Abs))
                    st(act.activation(w, w, ACT.Exp, scale=-1.0))
                    act.activation(w, w, ACT.Ln, bias=ones_col[0:4, 0:1]).then_inc(s["fl"], 1)
                elif name == "foxs":
                    softmax(L, 0, S0)
                elif name == "diffs0":
                    softmax(L, 1, S0)
                elif name == "diffs1":
                    softmax(L, 2, S1)
                elif name in ("foxt", "difft"):
                    turned_out(L, 0 if name == "foxt" else 1)
                elif name in ("gelu_u", "gelu_v"):
                    v = name == "gelu_v"
                    z, tmp = (zt["gv"], zt["fk"]) if v else (zt["gu"], zt["fq"])
                    copied(L, zi["gv" if v else "gu"])
                    act.wait_ge(s["scores"], seq(L, ROUNDS, 1))
                    act.activation(tmp, z, ACT.Square).then_inc(s["gu_sq"], 1)
                    act.wait_ge(s["gu_t"], 2 * l + (2 if v else 1))
                    act.activation(tmp, tmp, ACT.Exp, scale=GELU_B).then_inc(s["gu_e"], 1)
                elif name == "foxout":
                    act.wait_ge(s["pv"], seq(L, TURNS, 1))
                    used(L, k0 + len(ZU1) - 1)
                    act.activation(xo(6, 8), ps[:, PVB, :], ACT.Copy).then_inc(s["outh"], 1)
                elif name == "gmlp":
                    act.wait_ge(s["lnv"], l + 1)
                    st(act.activation(lnr[:, 0, :], lnmv[:, :, 1], ACT.Ln, bias=epsc[:, 0:1]))
                    act.activation(lnr[:, 0, :], lnr[:, 0, :], ACT.Exp, scale=-0.5).then_inc(s["lny"], 1)
                    act.wait_ge(s["gu"], l + 1)
                    act.activation(xo(4, 6), zt["gu"], ACT.Copy).then_inc(s["outh"], 1)
                elif name == "diffout":
                    act.wait_ge(s["pv"], seq(L, TURNS, 2))
                    act.activation(u8[:, 1536:2048], ps[:, PVB, :], ACT.Square).then_inc(s["sq"], 1)
                    rs(st, L.event(4), sq8[:, 1536:2048], ps[:, 6, :])
                    act.wait_ge(s["dout"], l + 1)
                    act.activation(xo(0, 2), s0f[:, 1024:1536], ACT.Copy).then_inc(s["outh"], 1)
                elif name == "convout":
                    act.wait_ge(s["craw"], l + 1)
                    act.activation(zt["cg"], zt["ca"], ACT.Square, scale=2.0).then_inc(s["sq"], 1)
                    rs(st, L.event(5), nrm[:, 0, :], ps[:, 3, 0:S])
                    act.wait_ge(s["cy"], 2 * l + 1)
                    act.activation(zt["cg"], zt["ca"], ACT.Exp, scale=-1.0).then_inc(s["cexp"], 1)
                    act.wait_ge(s["cy"], 2 * l + 2)
                    act.activation(xo(2, 4), zt["ca"], ACT.Copy).then_inc(s["outh"], 1)

            def stage2(L, st, k0, name):
                l = L.l
                if name == "silu":
                    copied(L, 3)
                    act.activation(sq8[:, :], HQG, ACT.Sigmoid).then_inc(s["sigm"], 1)
                elif name == "hprep":
                    z = HF[:, :, :].rearrange("p h t -> p (h t)")
                    copied(L, 5)
                    st(act.activation(u8h[0], z, ACT.Abs))
                    st(act.activation(u8h[0], u8h[0], ACT.Exp, scale=-1.0))
                    act.activation(u8h[0], u8h[0], ACT.Ln, bias=ones_col[:, 0:1]).then_inc(s["hz4"], 1)
                    act.wait_ge(s["hz1"], l + 1)
                    for h in range(4):
                        ins = act.activation(HK[:, h, :], u8h[0][:, h * S:h * S + S], ACT.Exp,
                                             bias=lbc[:, 1, h:h + 1])
                    ins.then_inc(s["hz2"], 1)
                    act.wait_ge(s["hz3"], l + 1)
                    st(act.activation(sq8h[0], sq8h[0], ACT.Abs))
                    st(act.activation(sq8h[0], sq8h[0], ACT.Exp, scale=-1.0))
                    act.activation(sq8h[0], sq8h[0], ACT.Ln, bias=ones_col[:, 0:1]).then_inc(s["hz4"], 1)
                elif name.startswith("lev") and name != "lev0":
                    n = int(name[3:])
                    b = 1 << (n - 1)
                    e = u8h[n % 2].rearrange("p (a b) -> p a b", b=2 * b)
                    act.wait_ge(s["ld"], l * 8 + n)
                    act.activation(e[:, :, 0:b], e[:, :, 0:b], ACT.Exp, scale=-1.0)
                    up = HC[:, :, P:S] if n == 8 else e[:, :, b:2 * b]
                    act.activation(e[:, :, b:2 * b], up, ACT.Exp).then_inc(s["le"], 1)
                elif name == "hlast":
                    act.wait_ge(s["hpv"], l + 1)
                    act.activation(HF[:, :, :].rearrange("p h t -> p (h t)"), stat2,
                                   ACT.Copy).then_inc(s["hsq"], 1)
                elif name in ("att0", "att1"):
                    softmax(L, int(name[-1]), S1, sink=True)
                elif name in ("attt0", "attt1"):
                    turned_out(L, int(name[-1]))
                elif name == "hout":
                    act.wait_ge(s["pv"], seq(L, TURNS, 2))
                    act.wait_ge(s["hsq"], l + 1)
                    act.activation(sq8h[0], HF[:, :, :].rearrange("p h t -> p (h t)"),
                                   ACT.Square).then_inc(s["sq"], 1)
                    rs(st, L.event(3), sq8h[1], hstat)
                    used(L, k0 + len(ZU2) - 1)
                    act.wait_ge(s["silu"], 2 * l + 2)
                    act.activation(xh[:, 0:4, :], HF[:, :, :], ACT.Copy).then_inc(s["outh"], 1)
                elif name == "attout":
                    act.activation(xh[:, 4:8, :].rearrange("p c t -> p (c t)"), stat2,
                                   ACT.Copy).then_inc(s["outh"], 1)
                elif name == "gates":
                    copied(L, len(ZU2) - 1)
                    ga = GA[:, :, :].rearrange("p c t -> p (c t)")
                    act.activation(ga, ga, ACT.Sigmoid).then_inc(s["gates"], 1)

            def mix(L, st, j, k0):
                units = ZU2 if L.b else ZU1
                plan, stage_of = (PLAN2, stage2) if L.b else (PLAN1, stage1)
                total = UNITS[("mix", L.b)]
                for i in range(total):
                    if i + 2 < total:
                        hi(L, k0 + i + 2)
                    if i < len(units):
                        used(L, k0 + i)
                        dst, src = z_dest(L.b, i), ps[:, i % 2, :]
                        if units[i][2] == "F":
                            dst, src = dst[:, 0:S], src[:, 0:S]
                        elif len(dst.shape) == 3:
                            src = src.rearrange("p (a b) -> p a b", a=2)
                        act.activation(dst, src, ACT.Copy).then_inc(z_copied[L.b], 1)
                    for name in plan.get(i, []):
                        stage_of(L, st, k0, name)
                    if L.b and i == 22:
                        used(L, k0 + 22)
                        for m in range(KC):
                            act.wait_ge(s["branch"], 2 * L.l + 1 + m // 4)
                            act.activation(xh[:, m, :], u8[:, m * S:m * S + S], ACT.Copy).then_inc(s["mixh"], 1)

            for blk in range(2):
                if not PARTS[blk]:
                    continue
                with act.Fori(0, LAYERS) as l:
                    L = Layer(blk, l)
                    st = Steps(act, act_step[blk], l, ACT_STEPS[blk])
                    for kind, j, k0, e in parts(blk):
                        norm(L, st, j, e, k0)
                        (ffn if kind == "ffn" else mix)(L, st, j, k0)
                        if j < len(PARTS[blk]) - 1:
                            hi(L, k0 + UNITS[(kind, blk)])
                        if blk:
                            post_norm(L, st, kind, j, e + {"ffn": 1, "mix": 2}[kind], k0 + UNITS[(kind, blk)] - 1)
                    assert st.k == ACT_STEPS[blk], ("ACT_STEPS", blk, st.k)

        @block.vector
        def _(dve):
            tt, ts, stt = dve.tensor_tensor, dve.tensor_scalar, dve.scalar_tensor_tensor
            st = Steps(dve, dve_setup)
            dve.drain().then_inc(lo_done, 3)
            dve.memset(ones_d[:, :], 1.0 / D)
            dve.memset(ones_128[:, :], 1.0 / P)
            dve.memset(ones_col[:, :], 1.0)
            dve.memset(ones_row[:, :], 1.0)
            dve.memset(epsc[:, :], EPS)
            dve.memset(zerow[:, :], 0.0)
            st(dve.memset(blk64[:, :], 0.0))
            for g in range(2):
                dve.memset(blk64[64 * g:64 * g + 64, 64 * g:64 * g + 64], 1.0 / 64)
            st(dve.memset(blk32[:, :], 0.0))
            for g in range(4):
                dve.memset(blk32[32 * g:32 * g + 32, 32 * g:32 * g + 32], 1.0 / 32)
            dve.memset(la[:, 0, :], NEG)
            dve.memset(l1[:, 0, :], 0.0)
            st(dve.memset(gB[:, :], 0.0))
            dve.wait_ge(stage_turned, 1)
            for t, n in enumerate(STAGE_ROWS):
                ins = dve.tensor_copy(prm[:, t * P:t * P + n], ps[:, 7, t * P:t * P + n])
            ins.then_inc(prm_ready, 1)
            for b in range(4):
                dve.wait_ge(x_turned, b + 1)
                dve.tensor_copy(hT[:, 2 * b:2 * b + 2, :].rearrange("p c t -> p (c t)"),
                                ps[:, b, :]).then_inc(h_ready, 2)
            dve.wait_ge(act_setup, 1)
            st(ts(condT[:, 1, :], condT[:, 0, :], 1.0, None, ALU.add))
            st(dve.reciprocal(condT[:, 1, :], condT[:, 1, :]))
            tt(condT[:, 2, :], condT[:, 1, :], prm[:, 120:128], ALU.mult).then_inc(cond_ready, 1)
            dve.wait_ge(cond_ready, 1)
            def ada_first(ks):
                for k in ks:
                    dve.wait_ge(ada0_loaded[k % 3], 16 * (k // 3 + 1))
                    if k == 0:
                        ins = ts(acc[:, 0, :], adaf[:, 0], condT[:, 2, 0:1], None, ALU.mult)
                    else:
                        dve.wait_ge(ada0_used, k)
                        ins = stt(acc[:, 0, :], adaf[:, k % 3], condT[:, 2, k:k + 1], acc[:, 0, :], ALU.mult, ALU.add)
                    ins.then_inc(ada0_used if k < KC - 1 else ada_ready[0], 1)

            ada_first(range(3))
            dve.wait_ge(consts_ready, 1)
            tri, gt = nrm[:, 0, 0:P], nrm[:, 1, 0:P]
            st(ts(tri, dist[:, 0:P], 0.0, None, ALU.is_le))
            st(ts(gt, dist[:, 0:P], 0.0, None, ALU.is_lt))
            for b in range(2):
                dve.wait_ge(ws_turned, b + 1)
                tt(wsT[:, 4 * b:4 * b + 4, :], ps[:, 4 + b, :].rearrange("p (h t) -> p h t", h=4),
                   tri.unsqueeze(1).to_broadcast([P, 4, P]), ALU.mult)
            xi, xf, ge = nrm[:, 2, 0:P].bitcast(I32), nrm[:, 2, P:2 * P], nrm[:, 1, P:2 * P]
            st(tt(xi, iot[:, 0:P], iot[:, P:2 * P], ALU.bitwise_xor))
            st(dve.tensor_copy(xf, xi))
            ts(hmask[:, 0, :], xf, 0.0, None, ALU.is_equal)
            st(tt(xf, xf, gt, ALU.mult))
            for n in range(1, 8):
                b = 1 << (n - 1)
                st(ts(ge, xf, float(b), None, ALU.is_ge))
                st(stt(hmask[:, n, :], xf, float(2 * b), ge, ALU.is_lt, ALU.mult))
            dve.wait_ge(smalls_loaded, SMALLS * 16)
            lv = lraw[:, :, :].rearrange("p (a b) d -> p a b d", b=2)
            st(tt(lprod[:, :, :], lv[:, :, 0, :], lv[:, :, 1, :], ALU.mult))
            dve.tensor_reduce(lamb[:, 0:4], lprod[:, :, :], AX.X, ALU.add).then_inc(s["lam"], 1)
            dve.wait_ge(act_setup, 2)
            for l in range(LAYERS):
                st(tt(lamb[:, 8 + l:9 + l], lamb[:, 4 + 2 * l:5 + 2 * l], lamb[:, 5 + 2 * l:6 + 2 * l], ALU.subtract))
                st(ts(lamb[:, 8 + l:9 + l], lamb[:, 8 + l:9 + l], LAM_INIT[l], None, ALU.add))
                st(ts(dog[:, l:l + 1], dog[:, l:l + 1], 1.0 - LAM_INIT[l], None, ALU.mult))
                st(ts(foxg[:, 2 * l:2 * l + 1], foxg[:, 2 * l:2 * l + 1], 0.125, None, ALU.mult))
            b0, b1 = prm[:, 212:216], prm[:, 216:220]
            st(tt(lbt[:, 4, :], b0, b1, ALU.max))
            st(tt(lbt[:, 0, :], b0, lbt[:, 4, :], ALU.subtract))
            tt(lbt[:, 1, :], b1, lbt[:, 4, :], ALU.subtract).then_inc(s["lam"], 1)
            dve.wait_ge(act_setup, 3)
            tt(lbt[:, 4, :], lbt[:, 2, :], lbt[:, 3, :], ALU.add).then_inc(s["lam"], 1)
            dve.wait_ge(act_setup, 4)
            tt(la[:, 1, :], lbt[:, 1, :], lbt[:, 5, :], ALU.subtract)
            tt(l1[:, 1, :], lbt[:, 0, :], lbt[:, 5, :], ALU.subtract).then_inc(dconsts_ready, 1)
            dve.wait_ge(dconsts_ready, 1)
            ada_first(range(3, KC))
            dve.wait_ge(ada_ready[0], 1)
            dve.drain().then_inc(ada1_used, 1)
            tt(sel[0:4, :, :], ident[0:4, 0:4].unsqueeze(2).to_broadcast([4, 4, S]),
               ident[0:4, 0:4].unsqueeze(2).to_broadcast([4, 4, S]), ALU.mult)

            def lo(L, k, i=0):
                dve.wait_ge(hi_done, L.unit(k, i) + 1)
                if L.b == 0 and unit_form(L, k) == "F":
                    a = [as8(t, k % 3)[:, :, 0:4] for t in (wlo, raw, whi)]
                else:
                    a = [t[:, k % 3, :] for t in (wlo, raw, whi)]
                tt(a[0], a[1], a[2].bitcast(F32), ALU.subtract).then_inc(lo_done, 1)

            def used(L, k, i=0):
                dve.wait_ge(unit_used, L.unit(k, i) + 4)

            def newton(st, e, ms, y, t, r):
                dve.wait_ge(y_ready, e + 1)
                st(tt(t, y, y, ALU.mult))
                st(stt(t, ms, EPS, t, ALU.add, ALU.mult))
                st(ts(t, t, -0.5, 1.5, ALU.mult, ALU.add))
                st(tt(r, y, t, ALU.mult))

            def norm(L, st, j, e, k0):
                n, l = L.sub(j), L.l
                if j == 0:
                    lo(L, k0)
                if L.b == 0:
                    dve.wait_ge(mod_summed, n + 1)
                    st(tt(mod[:, :], ps[:, 7, 0:24], prm[:, bass.ds(l * P + 24 * j, 24)], ALU.add))
                    st(stt(gA[:, :], mod[:, 8:16], 1.0, prm[:, bass.ds(l * 24 + (72 + 8 * j), 8)], ALU.add, ALU.mult))
                    st(dve.tensor_copy(gB[:, :], mod[:, 0:8]))
                    st(ts(gG[:, :], mod[:, 16:24], 1.0 if j == 1 else 0.5, None, ALU.mult))
                else:
                    st(dve.tensor_copy(gA[:, :], prm[:, bass.ds(l * 48 + (256 + 16 * j), 8)]))
                    st(dve.memset(gB[:, :], 0.0))
                    st(ts(gG[:, :], prm[:, bass.ds(l * 48 + (264 + 16 * j), 8)], 1.0 if j == 1 else 0.5, None, ALU.mult))
                newton(st, L.event(e), ps[:, STAT, 0:S], nrm[:, 0, :], nrm[:, 1, :], nrm[:, 2, :])
                for m in range(KC + 1):
                    if m < KC:
                        stt(u8[:, m * S:m * S + S], hT[:, m, :], gA[:, m:m + 1], nrm[:, 2, :], ALU.mult,
                            ALU.mult).then_inc(u_ready, 1)
                    if m:
                        dve.wait_ge(xh_ready, 8 * n + m)
                        stt(xl[:, m - 1, :], u8[:, m * S - S:m * S], gB[:, m - 1:m], xh[:, m - 1, :].bitcast(F32),
                            ALU.add, ALU.subtract).then_inc(x_ready, 1)
                lo(L, k0 + 1)

            def finish(L, st, kind, j, e, klast):
                if j < len(PARTS[L.b]) - 1:
                    lo(L, klast + 1)
                if L.b:
                    used(L, klast)
                    newton(st, L.event(e), ps[:, STAT, 0:S], nrm[:, 0, :], nrm[:, 1, :], nrm[:, 2, :])
                    for m in range(KC):
                        st(stt(u8[:, m * S:m * S + S], ps[:, ACC + m // 2, (m % 2) * S:(m % 2) * S + S], gG[:, m:m + 1],
                               nrm[:, 2, :], ALU.mult, ALU.mult))
                        tt(hT[:, m, :], hT[:, m, :], u8[:, m * S:m * S + S], ALU.add).then_inc(h_ready, 1)
                else:
                    for m in range(KC):
                        if m % 2 == 0:
                            bank_done(dve, L, kind, j, klast, m // 2)
                        stt(hT[:, m, :], ps[:, ACC + m // 2, (m % 2) * S:(m % 2) * S + S], gG[:, m:m + 1], hT[:, m, :],
                            ALU.mult, ALU.add).then_inc(h_ready, 1)

            def ffn(L, st, j, k0):
                g0 = L.ffn(j) * GROUPS

                def product(g, k, i=0):
                    dve.wait_ge(sig_ready, g0 + g + 1)
                    tt(sq8[:, 512:1024], ps[:, G_BANK, :], sq8[:, 0:512], ALU.mult).then_inc(prod_ready, 1)
                    dve.wait_ge(prod_ready, g0 + g + 1)
                    used(L, k, i)
                    tt(u8[:, 0:512], sq8[:, 512:1024], ps[:, U_BANK, :], ALU.mult).then_inc(h32_ready, 1)

                def rest(g):
                    dve.wait_ge(hidh_ready, g0 + g + 1)
                    tt(hidl[:, :], u8[:, 0:512], hidh[:, :].bitcast(F32), ALU.subtract).then_inc(hid_ready, 1)

                lo(L, k0 + 2)
                lo(L, k0 + 3)
                product(0, k0 + 1)
                rest(0)

                def ada(i, piece):
                    if piece == 0:
                        dve.wait_ge(ada1_loaded, 16 * (L.l * KC + i) + 16)
                    seg = slice(1024 * piece, 1024 * piece + 1024)
                    ins = stt(acc[:, 1, seg], adam[:, seg], condT[:, 2, bass.ds(i, 1)], acc[:, 1, seg],
                              ALU.mult, ALU.add)
                    if piece == 2:
                        ins.then_inc(ada1_used, 1)

                def group(i, with_ada=False):
                    lo(L, k0 + 4, i)
                    if with_ada:
                        ada(i, 0)
                    lo(L, k0 + 5, i)
                    if with_ada:
                        ada(i, 1)
                        ada(i, 2)
                    product(i + 1, k0 + 3, i)
                    lo(L, k0 + 6, i)
                    rest(i + 1)

                mixers = L.b == 0 and j == 0 and "mix" in PARTS[0]
                if mixers:
                    dve.memset(acc[:, 1, :], 0.0).then_inc(acc_zeroed, 1)
                    dve.wait_ge(acc_zeroed, L.l + 1)
                    dve.sem_inc(dve_waited, 1)
                    with dve.Fori(0, KC) as i:
                        group(i, True)
                    dve.drain().then_inc(ada_ready[1], 1)
                with dve.Fori(KC if mixers else 0, GROUPS - 2) as i:
                    group(i)
                k = k0 + 3 * (GROUPS - 2)
                lo(L, k + 4)
                lo(L, k + 5)
                product(GROUPS - 1, k + 3)
                rest(GROUPS - 1)

            def copied(L, i):
                dve.wait_ge(z_copied[L.b], L.l * NZ[L.b] + i + 1)

            def softmax(L, st, a, tile, mask, scale, g=None):
                dve.wait_ge(s["scores"], seq(L, ROUNDS, a + 1))
                stt(tile[:, :, 0:P], sc0, scale, mask[:, 0:P].unsqueeze(1).to_broadcast([P, 4, P]), ALU.mult, ALU.add)
                stt(tile[:, :, P:3 * P], sc1, scale, mask[:, P:3 * P].unsqueeze(1).to_broadcast([P, 4, 2 * P]),
                    ALU.mult, ALU.add).then_inc(s["scores_read"], 1)
                dve.wait_ge(s["scores_read"], seq(L, ROUNDS, a + 1))
                if g is not None:
                    for h in range(4):
                        ins = stt(tile[:, h, :], dist[:, :], -(2.0 ** -(4 * g + h + 1)), tile[:, h, :], ALU.mult, ALU.add)
                    st(ins)
                dve.tensor_reduce(mx[:, 0:4], tile[:, :, 0:P], AX.X, ALU.max)
                st(dve.tensor_reduce(mx[:, 4:8], tile[:, :, P:3 * P], AX.X, ALU.max))
                if g is not None:
                    sk = sinkb[:, bass.ds(L.l * 8 + 4 * g, 4)].unsqueeze(1).to_broadcast([P, 2, 4])
                    m2 = mx[:, :].rearrange("p (b h) -> p b h", b=2)
                    st(tt(m2, m2, sk, ALU.max))
                    tt(sinke[:, :].rearrange("p (b h) -> p b h", b=2), sk, m2, ALU.subtract)
                ts(nmx[:, :], mx[:, :], -1.0, None, ALU.mult).then_inc(s["nmax"], 1)
                dve.wait_ge(s["probs"], seq(L, ROUNDS, a + 1))
                if g is not None:
                    st(tt(ssum[:, :], ssum[:, :], sinke[:, :], ALU.add))
                st(dve.reciprocal(rsum[:, :], ssum[:, :]))

            def scaled(tile):
                r = rsum[:, :]
                return [(tile[:, :, a:b], r[:, c:c + 4].unsqueeze(2).to_broadcast([P, 4, b - a]))
                        for a, b, c in ((0, P, 0), (P, 3 * P, 4))]

            def rest_out(L, n, c0, c1, src):
                dve.wait_ge(s["outh"], seq(L, OUTS, n))
                tt(xl[:, c0:c1, :].rearrange("p c t -> p (c t)"), src,
                   xh[:, c0:c1, :].bitcast(F32).rearrange("p c t -> p (c t)"), ALU.subtract).then_inc(s["o"], 1)

            def gelu(L, st, z, tmp, n, done):
                dve.wait_ge(s["gu_sq"], 2 * L.l + n)
                st(ts(tmp, tmp, GELU_A, 1.0, ALU.mult, ALU.add))
                tt(tmp, tmp, z, ALU.mult).then_inc(s["gu_t"], 1)
                dve.wait_ge(s["gu_e"], 2 * L.l + n)
                st(ts(tmp, tmp, 1.0, None, ALU.add))
                st(dve.reciprocal(tmp, tmp))
                st(tt(z, z, tmp, ALU.mult))

            def stage1(L, st, k0, name):
                l = L.l
                ca2 = zt["ca"].rearrange("p (c t) -> p c t", c=2)
                if name == "convin":
                    dve.wait_ge(s["convexp"], l + 1)
                    st(ts(u8[:, 0:512], u8[:, 0:512], 1.0, None, ALU.add))
                    st(dve.reciprocal(u8[:, 0:512], u8[:, 0:512]))
                    dve.memset(ypad[:, :, 0:CONVK - 1], 0.0)
                    tt(ypad[:, :, CONVK - 1:], ca2, u8[:, 0:512].rearrange("p (c t) -> p c t", c=2),
                       ALU.mult).then_inc(s["conv_in"], 1)
                elif name in ("foxqk", "diffqk"):
                    q = 0 if name == "foxqk" else 1
                    newton(st, L.event(2 + q), stat2, sq8h[1], u8h[1], u8h[0])
                    gain = (foxg, diffg)[q]
                    for i, z in enumerate((zt["fq" if q == 0 else "dq"], zt["fk" if q == 0 else "dk"])):
                        ins = stt(z, z, gain[:, bass.ds(2 * l + i, 1)], u8[:, 512 * i:512 * i + 512], ALU.mult, ALU.mult)
                    ins.then_inc(s[name], 1)
                elif name == "foxf":
                    copied(L, zi["f"])
                    f, w = zt["f"][0:4, 0:S], zt["f"][0:4, S:2 * S]
                    ts(f, f, fb[0:4, bass.ds(l, 1)], None, ALU.add).then_inc(s["fx"], 1)
                    dve.wait_ge(s["fl"], l + 1)
                    st(stt(f, f, 0.0, w, ALU.min, ALU.subtract))
                    dve.tensor_tensor_scan(gcum[0:4, 0, 0:P], ones_row[0:4, :], f[:, 0:P], 0.0, ALU.mult, ALU.add)
                    st(dve.drain())
                    st(dve.tensor_tensor_scan(gcum[0:4, 0, P:S], ones_row[0:4, :], f[:, P:S], gcum[0:4, 0, P - 1:P],
                                              ALU.mult, ALU.add))
                    ts(gcum[0:4, 1, :], gcum[0:4, 0, :], -1.0, None, ALU.mult).then_inc(s["foxcum"], 1)
                elif name == "foxs":
                    softmax(L, st, 0, S0, amask, 1.0)
                    (a, ra), (b, rb) = scaled(S0)
                    tt(a, a, ra, ALU.mult)
                    tt(b, b, rb, ALU.mult).then_inc(s["pnorm"], 1)
                elif name == "diffs0":
                    dve.wait_ge(s["pturned"], seq(L, TURNS, 1))
                    softmax(L, st, 1, S0, amask, 32 ** -0.5)
                    (a, ra), (b, rb) = scaled(S0)
                    tt(a, a, ra, ALU.mult)
                    st(tt(b, b, rb, ALU.mult))
                elif name == "diffs1":
                    softmax(L, st, 2, S1, amask, 32 ** -0.5)
                    st(ts(rsum[:, :], rsum[:, :], lamb[:, bass.ds(l + 8, 1)], None, ALU.mult))
                    (a, ra), (b, rb) = scaled(S1)
                    tt(a, a, ra, ALU.mult)
                    st(tt(b, b, rb, ALU.mult))
                    tt(s0f, s0f, s1f, ALU.subtract).then_inc(s["pnorm"], 1)
                elif name == "gelu_u":
                    gelu(L, st, zt["gu"], zt["fq"], 1, None)
                elif name == "foxout":
                    rest_out(L, 1, 6, 8, ps[:, PVB, :])
                elif name == "gelu_v":
                    gelu(L, st, zt["gv"], zt["fk"], 2, None)
                elif name == "gmlp":
                    v = zt["gv"].rearrange("p (b e) -> p b e", b=2)
                    for b in range(2):
                        ins = dve.bn_stats(lnst[:, b, :], v[:, b, :])
                    st(ins)
                    dve.sem_inc(dve_waited, 1)
                    for b in range(2):
                        ins = dve.bn_aggr(lnmv[:, b, :], lnst[:, b, :])
                    ins.then_inc(s["lnv"], 1)
                    dve.wait_ge(s["lny"], l + 1)
                    st(tt(lnr[:, 1, :], lnr[:, 0, :], lnr[:, 0, :], ALU.mult))
                    st(stt(lnr[:, 1, :], lnmv[:, :, 1], EPS, lnr[:, 1, :], ALU.add, ALU.mult))
                    st(ts(lnr[:, 1, :], lnr[:, 1, :], -0.5, 1.5, ALU.mult, ALU.add))
                    st(tt(lnr[:, 2, :], lnr[:, 0, :], lnr[:, 1, :], ALU.mult))
                    for b in range(2):
                        ins = ts(v[:, b, :], v[:, b, :], lnmv[:, b, 0:1], lnr[:, 2, b:b + 1], ALU.subtract, ALU.mult)
                    st(ins)
                    st(dve.tensor_copy(zt["fq"].rearrange("p (h t) -> p h t", h=4), wsT[:, bass.ds(4 * l, 4), :]))
                    st(tt(v, v, ngb[:, 0, bass.ds(l, 1), :].to_broadcast([P, 2, 256]), ALU.mult))
                    tt(v, v, ngb[:, 1, bass.ds(l, 1), :].to_broadcast([P, 2, 256]), ALU.add).then_inc(s["gv"], 1)
                    dve.wait_ge(s["gmix"], l + 1)
                    t = zt["fk"].rearrange("p (c b t) -> p c b t", c=2, b=2)
                    m = ps[:, 7, :].rearrange("p (c b t) -> p c b t", c=2, b=2)
                    for b in range(2):
                        ins = tt(t[:, :, b, :], m[:, :, b, :],
                                 bsb[:, bass.ds(l, 1), :, :].rearrange("p l c t -> p (l c) t"), ALU.add)
                    st(ins)
                    tt(zt["gu"], zt["gu"], zt["fk"], ALU.mult).then_inc(s["gu"], 1)
                    rest_out(L, 2, 4, 6, zt["gu"])
                elif name == "diffout":
                    newton(st, L.event(4), ps[:, 6, :], sq8[:, 1536:2048], s0f[:, 0:512], s0f[:, 512:1024])
                    stt(s0f[:, 1024:1536], ps[:, PVB, :], dog[:, bass.ds(l, 1)], s0f[:, 512:1024], ALU.mult,
                        ALU.mult).then_inc(s["dout"], 1)
                    rest_out(L, 3, 0, 2, s0f[:, 1024:1536])
                elif name == "convout":
                    dve.wait_ge(s["cmean"], l + 1)
                    mean = ps[:, 2, 0:S].unsqueeze(1).to_broadcast([P, 2, S])
                    stt(ca2, mean, -4.0, ca2, ALU.mult, ALU.add).then_inc(s["craw"], 1)
                    newton(st, L.event(5), ps[:, 3, 0:S], nrm[:, 0, :], nrm[:, 1, :], nrm[:, 2, :])
                    st(tt(ca2, ca2, nrm[:, 2, :].unsqueeze(1).to_broadcast([P, 2, S]), ALU.mult))
                    for ch in range(2):
                        ins = ts(ca2[:, ch, :], ca2[:, ch, :], prm[:, bass.ds(2 * l + (P + 76 + ch), 1)],
                                 prm[:, bass.ds(2 * l + (P + 80 + ch), 1)], ALU.mult, ALU.add)
                    ins.then_inc(s["cy"], 1)
                    dve.wait_ge(s["cexp"], l + 1)
                    st(ts(zt["cg"], zt["cg"], 1.0, None, ALU.add))
                    st(dve.reciprocal(zt["cg"], zt["cg"]))
                    tt(zt["ca"], zt["ca"], zt["cg"], ALU.mult).then_inc(s["cy"], 1)
                    rest_out(L, 4, 2, 4, zt["ca"])

            def take(L, n):
                dve.wait_ge(s["lmm"], L.l * 9 + n + 1)
                if n == 8:
                    dve.tensor_copy(AT[:, 8:12, :].rearrange("p a t -> p (a t)"),
                                    lbank[0][:, 0:512]).then_inc(s["hz"], 1)
                else:
                    dve.sem_inc(dve_waited, 1)
                    dve.copy_predicated(AT[:, 0:8, :], hmask[:, n:n + 1, :].to_broadcast([P, 8, P]),
                                        lbank[n % 2].rearrange("p (a t) -> p a t", a=8))

            def stage2(L, st, k0, name):
                l = L.l
                if name == "silu":
                    dve.wait_ge(s["sigm"], l + 1)
                    tt(HQG, HQG, sq8[:, :], ALU.mult).then_inc(s["silu"], 1)
                elif name == "hprep":
                    flat = lambda t: t[:, :, :].rearrange("p h t -> p (h t)")
                    st(dve.tensor_copy(lbc[:, 0:1, :], la[:, bass.ds(l, 1), :]))
                    st(dve.tensor_copy(lbc[:, 1:2, :], l1[:, bass.ds(l, 1), :]))
                    dve.wait_ge(s["hz4"], 2 * l + 1)
                    st(stt(u8h[1], flat(HF), 0.0, u8h[0], ALU.min, ALU.subtract))
                    tt(u8h[0], u8h[1], flat(HF), ALU.subtract).then_inc(s["hz1"], 1)
                    dve.wait_ge(s["hz1"], l + 1)
                    dve.wait_ge(s["silu"], 2 * l + 1)
                    for h in range(4):
                        seg = slice(h * S, h * S + S)
                        ts(HF[:, h, :], u8h[1][:, seg], lbc[:, 1, h:h + 1], lbc[:, 0, h:h + 1], ALU.add, ALU.max)
                        ins = ts(sq8h[0][:, seg], u8h[1][:, seg], lbc[:, 1, h:h + 1], lbc[:, 0, h:h + 1], ALU.add,
                                 ALU.subtract)
                    ins.then_inc(s["hz3"], 1)
                    dve.wait_ge(s["hz3"], l + 1)
                    dve.wait_ge(s["hz4"], 2 * l + 2)
                    st(tt(flat(HF), flat(HF), sq8h[0], ALU.add))
                    for b in range(8):
                        seg = slice((b % 2) * P, (b % 2) * P + P)
                        ins = dve.tensor_tensor_scan(HC[:, b // 2, seg], ones_row[:, :], HF[:, b // 2, seg], 0.0,
                                                     ALU.mult, ALU.add)
                    dve.wait_ge(s["hz2"], l + 1)
                    dve.sem_inc(dve_waited, 1)
                    ins = dve.drain()
                    ins.then_inc(s["hcum"], 1)
                    dve.wait_ge(s["hcum"], l + 1)
                elif name.startswith("lev"):
                    n = int(name[3:])
                    if n == 0:
                        return
                    b = 1 << (n - 1)
                    hc = HC[:, :, :].rearrange("p h t -> p (h t)").rearrange("p (a b) -> p a b", b=2 * b)
                    hq = HQ[:, :, :].rearrange("p h t -> p (h t)").rearrange("p (a b) -> p a b", b=2 * b)
                    hk = HK[:, :, :].rearrange("p h t -> p (h t)").rearrange("p (a b) -> p a b", b=2 * b)
                    e = u8h[n % 2].rearrange("p (a b) -> p a b", b=2 * b)
                    xx = sq8h[n % 2].rearrange("p (a b) -> p a b", b=2 * b)
                    w = b if n == 8 else 2 * b
                    cnt = 1024 // (2 * b)
                    tt(e[:, :, 0:w], hc[:, :, 0:w], hc[:, :, b - 1:b].to_broadcast([P, cnt, w]),
                       ALU.subtract).then_inc(s["ld"], 1)
                    dve.wait_ge(s["le"], l * 8 + n)
                    if n >= 2:
                        dve.wait_ge(s["lmm"], l * 9 + n - 1)
                    tt(xx[:, :, 0:b], hk[:, :, 0:b], e[:, :, 0:b], ALU.mult)
                    tt(xx[:, :, b:2 * b], hq[:, :, b:2 * b], e[:, :, b:2 * b], ALU.mult).then_inc(s["lx"], 1)
                    take(L, n - 1)
                elif name == "hlast":
                    take(L, 8)
                elif name in ("att0", "att1"):
                    g = int(name[-1])
                    if g:
                        dve.wait_ge(s["pturned"], seq(L, TURNS, 1))
                    softmax(L, st, g, S1, wmask, 0.125, g)
                    (a, ra), (b, rb) = scaled(S1)
                    tt(a, a, ra, ALU.mult)
                    tt(b, b, rb, ALU.mult).then_inc(s["pnorm"], 1)
                elif name == "hout":
                    flat = HF[:, :, :].rearrange("p h t -> p (h t)")
                    newton(st, L.event(3), hstat, sq8h[1], u8h[0], u8h[1])
                    st(stt(flat, flat, prm[:, bass.ds(l + (P + 92), 1)], u8h[1], ALU.mult, ALU.mult))
                    tt(flat, flat, HG[:, :, :].rearrange("p h t -> p (h t)"), ALU.mult).then_inc(s["silu"], 1)
                    rest_out(L, 1, 0, 4, flat)
                elif name == "attout":
                    rest_out(L, 2, 4, 8, stat2)

            def branch(L, st, k0, n):
                used(L, k0 + 19 + n)
                dve.wait_ge(s["gates"], L.l + 1)
                gate = GA[:, 4 * n:4 * n + 4, :].rearrange("p c t -> p (c t)")
                if n < 2:
                    st(tt(u8h[n], br_bank[n], gate, ALU.mult))
                else:
                    st(tt(sq8h[n % 2], br_bank[n], gate, ALU.mult))
                    tt(u8h[n % 2], u8h[n % 2], sq8h[n % 2], ALU.add).then_inc(s["branch"], 1)

            def mix(L, st, j, k0):
                plan, stage_of = (PLAN2, stage2) if L.b else (PLAN1, stage1)
                total = UNITS[("mix", L.b)]
                for i in range(total):
                    if i + 2 < total:
                        lo(L, k0 + i + 2)
                    for name in plan.get(i, []):
                        stage_of(L, st, k0, name)
                    if L.b and 19 <= i < 23:
                        branch(L, st, k0, i - 19)
                    if L.b and i == 22:
                        for m in range(KC):
                            dve.wait_ge(s["mixh"], 8 * L.l + m + 1)
                            tt(xl[:, m, :], u8[:, m * S:m * S + S], xh[:, m, :].bitcast(F32),
                               ALU.subtract).then_inc(s["mixed"], 1)

            for blk in range(2):
                if not PARTS[blk]:
                    continue
                if blk and "mix" in PARTS[1]:
                    dve.memset(AT[:, :, :], 0.0)
                with dve.Fori(0, LAYERS) as l:
                    L = Layer(blk, l)
                    st = Steps(dve, dve_step[blk], l, DVE_STEPS[blk])
                    for kind, j, k0, e in parts(blk):
                        norm(L, st, j, e, k0)
                        (ffn if kind == "ffn" else mix)(L, st, j, k0)
                        finish(L, st, kind, j, e + {("ffn", 0): 0, ("mix", 0): 0, ("ffn", 1): 1, ("mix", 1): 2}[(kind, blk)],
                               k0 + UNITS[(kind, blk)] - 1)
                    assert st.k == DVE_STEPS[blk], ("DVE_STEPS", blk, st.k)
            dve.wait_ge(x_turned, 5)
            for b in range(4):
                ins = dve.tensor_copy(sq8[:, b * 512:b * 512 + 512], ps[:, b, :])
            ins.then_inc(y_out, 1)

        @block.gpsimd
        def _(pool):
            st = Steps(pool, pool_step)
            st(pool.memset(ident[:, :], 0.0))
            st(pool.affine_select(out=ident[:, :], in_=ident[:, :], compare_op=ALU.not_equal, fill=1.0, base=0,
                                  pattern=[[-1, P]], channel_multiplier=1))
            st(pool.memset(amask[:, :], 0.0))
            st(pool.memset(wmask[:, :], 0.0))
            for mask in (amask, wmask):
                for at in (0, 2 * P):
                    st(pool.affine_select(out=mask[:, at:at + P], in_=mask[:, at:at + P], compare_op=ALU.is_ge,
                                          fill=NEG, base=0, pattern=[[-1, P]], channel_multiplier=1))
            st(pool.affine_select(out=wmask[:, P:2 * P], in_=wmask[:, P:2 * P], compare_op=ALU.is_gt, fill=NEG,
                                  base=0, pattern=[[1, P]], channel_multiplier=-1))
            st(pool.iota(iot[:, 0:P], pattern=[[-1, P]], base=0, channel_multiplier=1))
            st(pool.iota(iot[:, P:3 * P], pattern=[[-1, 2 * P]], base=P, channel_multiplier=1))
            st(pool.tensor_copy(dist[:, :], iot[:, 0:3 * P]))
            st(pool.iota(iot[:, 0:P], pattern=[[0, P]], base=0, channel_multiplier=1))
            st(pool.iota(iot[:, P:2 * P], pattern=[[1, P]], base=0, channel_multiplier=0))
            pool.drain().then_inc(consts_ready, 1)
            if not PARTS[0]:
                return
            pool.wait_ge(cond_ready, 1)
            pool.wait_ge(dconsts_ready, 1)
            pool.wait_ge(ws_turned, 2)
            cols = adaT.shape[2]
            PIECES = 3072 // cols

            def until(sem_, value):
                pool.wait_ge(sem_, value)
                pool.sem_inc(pool_waited, 1)

            def ada(n, l, j):
                sums = acc[:, j % 2, :]
                w = ada_w[l].rearrange("(c p) n -> c p n", p=P)

                def load(i, piece):
                    src = w[bass.ds(i, 1), :, 3072 * j + cols * piece:3072 * j + cols * piece + cols]
                    pool.dma_start(adaT[:, piece % 2, :], src.rearrange("c p n -> p (c n)")
                                   ).then_inc(ada_loaded[piece % 2], 16)

                pool.memset(sums, 0.0).then_inc(ada_zeroed, 1)
                pool.wait_ge(ada_zeroed, n + 1)
                load(0, 0)
                load(0, 1)

                def chunk(i, last):
                    done = (n * KC + i) * PIECES
                    pool.tensor_copy(condk[:, :], condT[:, 2, bass.ds(i, 1)]).then_inc(condk_ready, 1)
                    until(condk_ready, n * KC + i + 1)
                    for piece in range(PIECES):
                        tile, part = adaT[:, piece % 2, :], sums[:, cols * piece:cols * piece + cols]
                        until(ada_loaded[piece % 2], (n * KC + i) * (8 * PIECES) + 16 * (piece // 2 + 1))
                        pool.tensor_scalar(tile, tile, condk[:, 0:1], 0.0, ALU.mult, ALU.add).then_inc(ada_scaled, 1)
                        until(ada_scaled, done + piece + 1)
                        pool.tensor_tensor(part, part, tile, ALU.add).then_inc(ada_added, 1)
                        until(ada_added, done + piece + 1)
                        if piece < PIECES - 2:
                            load(i, piece + 2)
                        elif not last:
                            load(i + 1, piece + 2 - PIECES)

                with pool.Fori(0, KC - 1) as i:
                    chunk(i, False)
                chunk(KC - 1, True)
                pool.drain().then_inc(ada_ready[j], 1)

            for l in range(LAYERS):
                if "mix" in PARTS[0]:
                    pool.wait_ge(mod_summed, len(PARTS[0]) * l + 1)
                    if len(PARTS[0]) == 3:
                        ada(2 * l, l, 2)
                    pool.wait_ge(s["conv_in"], l + 1)
                    for tap in range(CONVK):
                        for ch in range(2):
                            w = prm[:, 384 + 62 * l + 2 * tap + ch:385 + 62 * l + 2 * tap + ch]
                            y, o = ypad[:, ch, tap:tap + S], zt["ca"][:, ch * S:ch * S + S]
                            t = zt["cg"][:, ch * S:ch * S + S]
                            if tap:
                                st(pool.tensor_scalar(t, y, w, 0.0, ALU.mult, ALU.add))
                                st(pool.tensor_tensor(o, o, t, ALU.add))
                            else:
                                bias = prm[:, P + 72 + 2 * l + ch:P + 73 + 2 * l + ch]
                                st(pool.tensor_scalar(o, y, w, bias, ALU.mult, ALU.add))
                    pool.drain().then_inc(s["conv_done"], 1)
                if l == 0:
                    pool.wait_ge(mod_summed, len(PARTS[0]) if len(PARTS[0]) != 2 else 1)
                    ada(1 if len(PARTS[0]) == 3 else 0, 1, 0)


_INS = ["x", "c", "ada_w", "ada_b", "norm_g", "ffn1_w_in", "ffn1_w_out", "ffn2_w_in", "ffn2_w_out", "w_in", "w_out",
        "diff_qk_g", "diff_lambda", "diff_out_g", "conv_w", "conv_b", "conv_norm_g", "conv_norm_b", "gmlp_norm_g",
        "gmlp_norm_b", "gmlp_ws", "gmlp_bs", "fox_qk_g", "fox_fb", "norm_gains_2", "w_ffn1_gate_2", "w_ffn1_up_2",
        "w_ffn1_down_2", "w_in_2", "hgrn_lower_bounds_2", "hgrn_head_gain_2", "attn_sinks_2", "w_branch_hgrn_2",
        "w_branch_attn_2", "w_out_2", "w_ffn2_gate_2", "w_ffn2_up_2", "w_ffn2_down_2"]


def kernel(**inputs):
    import numpy as _np
    import concourse.bacc as _bacc
    from concourse import mybir as _mybir
    from concourse.bass_utils import run_bass_kernel_spmd as _run

    nc = _bacc.Bacc("TRN2", target_bir_lowering=False, num_devices=1)
    arrays, args = {}, []
    for name in _INS:
        a = _np.ascontiguousarray(inputs[name])
        arrays[f"in_{name}_dram"] = a
        args.append(nc.dram_tensor(f"in_{name}_dram", a.shape, _mybir.dt.from_np(a.dtype), kind="ExternalInput").ap())
    args.append(nc.dram_tensor("out_0_dram", (1, 256, 1024), _mybir.dt.from_np(_np.dtype("float32")),
                               kind="ExternalOutput").ap())
    program(nc, *args)
    r = _run(nc, [arrays], core_ids=[0])
    return r.results[0]["out_0_dram"]
```
